# Optimizing a Trainium2 kernel written in Bass

```python
import math
import jax, jax.numpy as jnp
from jax import lax
import numpy as np

D_MODEL = 1024
BATCH = 1
SEQ = 512
DEPTH = 2

HEAD_DIM = 64
A_Q_HEADS = 8
A_KV_HEADS = 2
WINDOW = 128
ROPE_DIM = HEAD_DIM // 4
ROPE_THETA = 500000.0
B_HEADS = 4
B_DK = 64
B_DV = 64
C_HEADS = 4
C_DK = 64
C_DV = 64
CONV_WIDTH = 4
CHUNK = 64
D_FF = -(-8 * D_MODEL // (3 * 256)) * 256
D_MIX = A_Q_HEADS * HEAD_DIM + B_HEADS * B_DV + C_HEADS * C_DV
C_CONV_CH = C_HEADS * (2 * C_DK + C_DV)
IN_SIZES = (A_Q_HEADS * HEAD_DIM, A_KV_HEADS * HEAD_DIM, A_KV_HEADS * HEAD_DIM,
            B_HEADS * B_DK, B_HEADS * B_DK, B_HEADS * B_DV, B_HEADS * B_DV,
            C_CONV_CH, C_HEADS * C_DV, C_HEADS, C_HEADS)
D_IN = sum(IN_SIZES)
NORM_EPS = 1e-6


def rmsnorm(x, gain):
    xf = x.astype(jnp.float32)
    y = xf * lax.rsqrt(jnp.mean(xf * xf, axis=-1, keepdims=True) + NORM_EPS)
    return (y * gain.astype(jnp.float32)).astype(x.dtype)

def l2norm(x):
    return x * lax.rsqrt(jnp.sum(x * x, axis=-1, keepdims=True) + NORM_EPS)

def partial_rope(x, positions):
    half = ROPE_DIM // 2
    inv_freq = ROPE_THETA ** (-jnp.arange(half, dtype=jnp.float32) * 2.0 / ROPE_DIM)
    ang = positions.astype(jnp.float32)[..., None] * inv_freq
    cos = jnp.cos(ang)[:, :, None, :]
    sin = jnp.sin(ang)[:, :, None, :]
    xf = x.astype(jnp.float32)
    x1, x2, xp = xf[..., :half], xf[..., half:ROPE_DIM], xf[..., ROPE_DIM:]
    out = jnp.concatenate([x1 * cos - x2 * sin, x2 * cos + x1 * sin, xp], axis=-1)
    return out.astype(x.dtype)

def sliding_window_attention(q, k, v, sinks):
    b, s, hq, d = q.shape
    hkv = k.shape[2]
    grp = hq // hkv
    nb = s // WINDOW
    qb = q.reshape(b, nb, WINDOW, hkv, grp, d)

    def band(t):
        tb = t.reshape(b, nb, WINDOW, hkv, d)
        prev = jnp.concatenate([jnp.zeros_like(tb[:, :1]), tb[:, :-1]], axis=1)
        return jnp.concatenate([prev, tb], axis=2)

    kb, vb = band(k), band(v)
    scores = jnp.einsum('bnqhgd,bnkhd->bnhgqk', qb, kb).astype(jnp.float32) * (d ** -0.5)
    qi = jnp.arange(WINDOW)[:, None]
    kj = jnp.arange(2 * WINDOW)[None, :]
    delta = qi + WINDOW - kj
    blk = jnp.arange(nb)[:, None, None]
    valid = (delta >= 0) & (delta < WINDOW) & (blk * WINDOW + kj - WINDOW >= 0)
    scores = jnp.where(valid[None, :, None, None], scores, -jnp.inf)
    sink = sinks.astype(jnp.float32).reshape(hkv, grp)[None, None, :, :, None, None]
    m = jnp.maximum(scores.max(axis=-1, keepdims=True), sink)
    p = jnp.exp(scores - m)
    denom = p.sum(axis=-1, keepdims=True) + jnp.exp(sink - m)
    out = jnp.einsum('bnhgqk,bnkhd->bnqhgd', (p / denom).astype(v.dtype), vb)
    return out.reshape(b, s, hq * d)

def hgrn2_chunked(q, log_f, v):
    b, s, h, dk = q.shape
    dv = v.shape[-1]
    nc = s // CHUNK

    def to_chunks(t):
        return t.reshape(b, nc, CHUNK, h, t.shape[-1]).transpose(1, 0, 3, 2, 4)

    causal = jnp.tril(jnp.ones((CHUNK, CHUNK), dtype=bool))

    def step(state, inp):
        qt, lf, vt = inp
        kt = -jnp.expm1(lf)
        cum = jnp.cumsum(lf, axis=2)
        diff = cum[:, :, :, None, :] - cum[:, :, None, :, :]
        decay = jnp.exp(jnp.where(causal[:, :, None], diff, -jnp.inf))
        attn = jnp.einsum('bhtd,bhsd,bhtsd->bhts', qt, kt, decay)
        o = attn @ vt + jnp.einsum('bhtd,bhde->bhte', qt * jnp.exp(cum), state)
        last = cum[:, :, -1:, :]
        state = jnp.exp(last[:, :, 0, :, None]) * state + jnp.einsum('bhsd,bhse->bhde', kt * jnp.exp(last - cum), vt)
        return state, o

    state0 = jnp.zeros((b, h, dk, dv), jnp.float32)
    _, o = lax.scan(step, state0, (to_chunks(q), to_chunks(log_f), to_chunks(v)))
    return o.transpose(1, 0, 3, 2, 4).reshape(b, s, h, dv)

def causal_depthwise_conv(x, w):
    ch = x.shape[-1]
    return lax.conv_general_dilated(x, w[:, None, :].astype(x.dtype), window_strides=(1,),
                                    padding=[(CONV_WIDTH - 1, 0)],
                                    dimension_numbers=('NWC', 'WIO', 'NWC'),
                                    feature_group_count=ch)

def gated_delta_chunked(q, k, v, beta, g):
    b, s, h, dk = q.shape
    dv = v.shape[-1]
    nc = s // CHUNK

    def to_chunks(t):
        return jnp.swapaxes(t.reshape((b, nc, CHUNK) + t.shape[2:]), 2, 3)

    qc, kc, vc, bc, gc = (to_chunks(t) for t in (q, k, v, beta, g))
    G = jnp.cumsum(gc, axis=-1)
    incl = jnp.tril(jnp.ones((CHUNK, CHUNK), dtype=bool))
    strict = jnp.tril(jnp.ones((CHUNK, CHUNK), dtype=bool), k=-1)
    L = jnp.exp(jnp.where(incl, G[..., :, None] - G[..., None, :], -jnp.inf))
    kb = kc * bc[..., None]
    A = jnp.where(strict, jnp.einsum('bnhtd,bnhsd->bnhts', kb, kc) * L, 0.0)
    eye = jnp.eye(CHUNK, dtype=jnp.float32)
    T = lax.linalg.triangular_solve(eye + A, jnp.broadcast_to(eye, A.shape), left_side=True,
                                    lower=True, unit_diagonal=True)
    U = T @ (vc * bc[..., None])
    W = T @ (kb * jnp.exp(G)[..., None])
    qk = jnp.where(incl, jnp.einsum('bnhtd,bnhsd->bnhts', qc, kc) * L, 0.0)
    q_dec = qc * jnp.exp(G)[..., None]
    k_dec = kc * jnp.exp(G[..., -1:] - G)[..., None]
    g_last = jnp.exp(G[..., -1])

    def step(state, inp):
        u, w, qd, kd, qkc, gl = inp
        v_new = u - w @ state
        o = qd @ state + qkc @ v_new
        state = gl[..., None, None] * state + jnp.swapaxes(kd, -1, -2) @ v_new
        return state, o

    xs = tuple(jnp.moveaxis(t, 1, 0) for t in (U, W, q_dec, k_dec, qk, g_last))
    state0 = jnp.zeros((b, h, dk, dv), jnp.float32)
    _, o = lax.scan(step, state0, xs)
    return jnp.swapaxes(jnp.moveaxis(o, 0, 1), 2, 3).reshape(b, s, h, dv)

def hybrid_mixer(h, positions, w_in, q_norm, k_norm, sinks, lb, hgrn_norm, conv_w, a_log, dt_bias,
                 gdn_norm, w_out):
    b, s, _ = h.shape
    f32 = jnp.float32
    proj = h @ w_in
    split_at = [int(i) for i in np.cumsum(IN_SIZES)[:-1]]
    aq, ak, av, bq, bf, bv, bg, cqkv, cg, cb, ca = jnp.split(proj, split_at, axis=-1)

    aq = partial_rope(rmsnorm(aq.reshape(b, s, A_Q_HEADS, HEAD_DIM), q_norm), positions)
    ak = partial_rope(rmsnorm(ak.reshape(b, s, A_KV_HEADS, HEAD_DIM), k_norm), positions)
    av = av.reshape(b, s, A_KV_HEADS, HEAD_DIM)
    out_a = sliding_window_attention(aq, ak, av, sinks)

    lb = lb.astype(f32).reshape(B_HEADS, B_DK)
    z = bf.reshape(b, s, B_HEADS, B_DK).astype(f32)
    log_f = jnp.logaddexp(jnp.log(lb), jnp.log1p(-lb) + jax.nn.log_sigmoid(z))
    o_b = hgrn2_chunked(bq.reshape(b, s, B_HEADS, B_DK).astype(f32), log_f,
                        bv.reshape(b, s, B_HEADS, B_DV).astype(f32))
    out_b = rmsnorm(o_b, hgrn_norm) * jax.nn.silu(bg.reshape(b, s, B_HEADS, B_DV).astype(f32))
    out_b = out_b.reshape(b, s, B_HEADS * B_DV).astype(h.dtype)

    cqkv = jax.nn.silu(causal_depthwise_conv(cqkv, conv_w))
    cq, ck, cv = jnp.split(cqkv, [C_HEADS * C_DK, 2 * C_HEADS * C_DK], axis=-1)
    cq = l2norm(cq.reshape(b, s, C_HEADS, C_DK).astype(f32)) * (C_DK ** -0.5)
    ck = l2norm(ck.reshape(b, s, C_HEADS, C_DK).astype(f32))
    cv = cv.reshape(b, s, C_HEADS, C_DV).astype(f32)
    beta = jax.nn.sigmoid(cb.astype(f32))
    g = -jnp.exp(a_log.astype(f32)) * jax.nn.softplus(ca.astype(f32) + dt_bias.astype(f32))
    o_c = gated_delta_chunked(cq, ck, cv, beta, g)
    out_c = rmsnorm(o_c, gdn_norm) * jax.nn.silu(cg.reshape(b, s, C_HEADS, C_DV).astype(f32))
    out_c = out_c.reshape(b, s, C_HEADS * C_DV).astype(h.dtype)

    mixed = jnp.concatenate([out_a, out_b, out_c], axis=-1)
    return mixed @ w_out

def swiglu(h, w_gate, w_up, w_down):
    return (jax.nn.silu(h @ w_gate) * (h @ w_up)) @ w_down

def first_inputs(seed: int = 0) -> dict:
    key = jax.random.key(seed)
    ks = jax.random.split(key, 24)
    f32 = jnp.float32

    def nrm(k, shape, scale):
        return jax.random.normal(k, shape, f32) * scale

    x = nrm(ks[0], (BATCH, SEQ, D_MODEL), 1.0)
    c = nrm(ks[1], (BATCH, D_MODEL), 1.0)
    positions = jnp.broadcast_to(jnp.arange(SEQ, dtype=jnp.int32)[None, :], (BATCH, SEQ))
    ada_w = nrm(ks[2], (DEPTH, D_MODEL, 6 * D_MODEL), 0.5 * D_MODEL ** -0.5)
    ada_b = nrm(ks[3], (DEPTH, 6 * D_MODEL), 0.02)
    norm_mix = 1.0 + nrm(ks[4], (DEPTH, D_MODEL), 0.05)
    w_in = nrm(ks[5], (DEPTH, D_MODEL, D_IN), D_MODEL ** -0.5)
    attn_q_norm = 1.0 + nrm(ks[6], (DEPTH, HEAD_DIM), 0.05)
    attn_k_norm = 1.0 + nrm(ks[7], (DEPTH, HEAD_DIM), 0.05)
    attn_sinks = nrm(ks[8], (DEPTH, A_Q_HEADS), 1.0)
    hgrn_lb_logits = nrm(ks[9], (DEPTH, B_HEADS * B_DK), 1.0)
    hgrn_out_norm = 1.0 + nrm(ks[10], (DEPTH, B_DV), 0.05)
    gdn_conv_w = nrm(ks[11], (DEPTH, CONV_WIDTH, C_CONV_CH), CONV_WIDTH ** -0.5)
    gdn_a_log = jnp.log(jax.random.uniform(ks[12], (DEPTH, C_HEADS), f32, 1.0, 16.0))
    dt = jnp.exp(jax.random.uniform(ks[13], (DEPTH, C_HEADS), f32, math.log(1e-3), math.log(1e-1)))
    gdn_dt_bias = dt + jnp.log(-jnp.expm1(-dt))
    gdn_out_norm = 1.0 + nrm(ks[14], (DEPTH, C_DV), 0.05)
    w_out = nrm(ks[15], (DEPTH, D_MIX, D_MODEL), D_MIX ** -0.5)
    norm_ffn = 1.0 + nrm(ks[16], (DEPTH, D_MODEL), 0.05)
    w_gate = nrm(ks[17], (DEPTH, D_MODEL, D_FF), D_MODEL ** -0.5)
    w_up = nrm(ks[18], (DEPTH, D_MODEL, D_FF), D_MODEL ** -0.5)
    w_down = nrm(ks[19], (DEPTH, D_FF, D_MODEL), D_FF ** -0.5)
    return {'x': x, 'c': c, 'positions': positions, 'ada_w': ada_w, 'ada_b': ada_b,
            'norm_mix': norm_mix, 'w_in': w_in, 'attn_q_norm': attn_q_norm,
            'attn_k_norm': attn_k_norm, 'attn_sinks': attn_sinks, 'hgrn_lb_logits': hgrn_lb_logits,
            'hgrn_out_norm': hgrn_out_norm, 'gdn_conv_w': gdn_conv_w, 'gdn_a_log': gdn_a_log,
            'gdn_dt_bias': gdn_dt_bias, 'gdn_out_norm': gdn_out_norm, 'w_out': w_out,
            'norm_ffn': norm_ffn, 'w_gate': w_gate, 'w_up': w_up, 'w_down': w_down}

def first_block(x, c, positions, ada_w, ada_b, norm_mix, w_in, attn_q_norm, attn_k_norm, attn_sinks,
              hgrn_lb_logits, hgrn_out_norm, gdn_conv_w, gdn_a_log, gdn_dt_bias, gdn_out_norm, w_out,
              norm_ffn, w_gate, w_up, w_down):
    lb_cum = jnp.cumsum(jax.nn.softmax(hgrn_lb_logits.astype(jnp.float32), axis=0), axis=0)
    lower_bounds = lb_cum - lb_cum[:1]
    cond = jax.nn.silu(c)
    for l in range(DEPTH):
        mod = cond @ ada_w[l] + ada_b[l]
        sh_m, sc_m, gt_m, sh_f, sc_f, gt_f = [m[:, None, :] for m in jnp.split(mod, 6, axis=-1)]
        h = rmsnorm(x, norm_mix[l]) * (1 + sc_m) + sh_m
        y = hybrid_mixer(h, positions, w_in[l], attn_q_norm[l], attn_k_norm[l], attn_sinks[l],
                         lower_bounds[l], hgrn_out_norm[l], gdn_conv_w[l], gdn_a_log[l],
                         gdn_dt_bias[l], gdn_out_norm[l], w_out[l])
        x = x + gt_m * y
        h = rmsnorm(x, norm_ffn[l]) * (1 + sc_f) + sh_f
        x = x + gt_f * swiglu(h, w_gate[l], w_up[l], w_down[l])
    return x


SSD_EXPAND = 2
SSD_INNER = SSD_EXPAND * D_MODEL
SSD_HEAD_DIM = 64
SSD_HEADS = SSD_INNER // SSD_HEAD_DIM
SSD_GROUPS = 4
SSD_STATE = 128
SSD_CONV = 5
SSD_CHUNK = 128
SSD_CONV_CH = SSD_INNER + 2 * SSD_GROUPS * SSD_STATE

DIFF_HEAD_DIM = 64
DIFF_HEADS = D_MODEL // (2 * DIFF_HEAD_DIM)
DIFF_WIDTH = DIFF_HEADS * 2 * DIFF_HEAD_DIM
Q_BLOCK = 128
ROPE_THETA_2 = 10000.0

MEM_TOKENS = 256
CROSS_HEADS = 4
CROSS_HEAD_DIM = D_MODEL // CROSS_HEADS
CROSS_WIDTH = CROSS_HEADS * CROSS_HEAD_DIM

N_BRANCH = 3
IN_COLS = (SSD_INNER + SSD_CONV_CH + 2 * SSD_HEADS + 4 * DIFF_WIDTH
           + 2 * CROSS_WIDTH + N_BRANCH * D_MODEL)
DEEPNORM_ALPHA = (2 * DEPTH) ** 0.25
DEEPNORM_BETA = (8 * DEPTH) ** -0.25
NORM_EPS_2 = 1e-5


def _in_splits():
    sizes = [SSD_INNER, SSD_CONV_CH, 2 * SSD_HEADS,
             DIFF_WIDTH, DIFF_WIDTH, DIFF_WIDTH, DIFF_WIDTH,
             CROSS_WIDTH, CROSS_WIDTH]
    return [int(v) for v in np.cumsum(sizes)]

def _rmsnorm(t, w):
    tf = t.astype(jnp.float32)
    tf = tf * lax.rsqrt(jnp.mean(tf * tf, axis=-1, keepdims=True) + NORM_EPS_2)
    return tf * w.astype(jnp.float32)

def _layernorm(t, g, b):
    tf = t.astype(jnp.float32)
    mu = jnp.mean(tf, axis=-1, keepdims=True)
    var = jnp.mean(jnp.square(tf - mu), axis=-1, keepdims=True)
    return (tf - mu) * lax.rsqrt(var + NORM_EPS_2) * g.astype(jnp.float32) + b.astype(jnp.float32)

def _rope_tables(positions):
    inv = 1.0 / (ROPE_THETA_2 ** (jnp.arange(0, DIFF_HEAD_DIM, 2, dtype=jnp.float32) / DIFF_HEAD_DIM))
    ang = positions.astype(jnp.float32)[..., None] * inv
    return jnp.cos(ang), jnp.sin(ang)

def _apply_rope(t, cos, sin):
    half = DIFF_HEAD_DIM // 2
    tf = t.astype(jnp.float32)
    t1, t2 = tf[..., :half], tf[..., half:]
    c = cos[:, :, None, None, :]
    s = sin[:, :, None, None, :]
    return jnp.concatenate([t1 * c - t2 * s, t1 * s + t2 * c], axis=-1)

def _centred_dwconv(t, w, b):
    pad = SSD_CONV // 2
    out = lax.conv_general_dilated(
        t, w[:, None, :].astype(t.dtype), window_strides=(1,),
        padding=[(pad, pad)], dimension_numbers=('NWC', 'WIO', 'NWC'),
        feature_group_count=t.shape[-1])
    return out + b.astype(t.dtype)

def _ssd_scan(xs, a, bm, cm):
    Bsz, L, H, P = xs.shape
    G, N = bm.shape[2], bm.shape[3]
    R = H // G
    Q = SSD_CHUNK
    C = L // Q
    xs = xs.astype(jnp.float32).reshape(Bsz, C, Q, G, R, P)
    bm = bm.astype(jnp.float32).reshape(Bsz, C, Q, G, N)
    cm = cm.astype(jnp.float32).reshape(Bsz, C, Q, G, N)
    a = a.astype(jnp.float32).reshape(Bsz, C, Q, G, R).transpose(0, 3, 4, 1, 2)
    a_cum = jnp.cumsum(a, axis=-1)
    lower = jnp.tril(jnp.ones((Q, Q), dtype=bool))
    seg = a_cum[..., :, None] - a_cum[..., None, :]
    decay = jnp.exp(jnp.where(lower, seg, -jnp.inf))
    y_diag = jnp.einsum('bcqgn,bcsgn,bgrcqs,bcsgrp->bcqgrp', cm, bm, decay, xs)
    decay_states = jnp.exp(a_cum[..., -1:] - a_cum)
    states = jnp.einsum('bcqgn,bgrcq,bcqgrp->bcgrpn', bm, decay_states, xs)
    chunk_decay = jnp.moveaxis(jnp.exp(a_cum[..., -1]), -1, 0)
    def step(h, inp):
        s_c, d_c = inp
        return h * d_c[..., None, None] + s_c, h
    h0 = jnp.zeros((Bsz, G, R, P, N), jnp.float32)
    _, prev = lax.scan(step, h0, (jnp.moveaxis(states, 1, 0), chunk_decay))
    prev = jnp.moveaxis(prev, 0, 1)
    y_off = jnp.einsum('bcqgn,bcgrpn,bgrcq->bcqgrp', cm, prev, jnp.exp(a_cum))
    return (y_diag + y_off).reshape(Bsz, L, H, P)

def _ssd_branch(z, xbc, dt_raw, conv_w, conv_b, dt_bias, a_log, d_skip, norm_w):
    Bsz, L, _ = z.shape
    gn = SSD_GROUPS * SSD_STATE
    xbc = jax.nn.silu(_centred_dwconv(xbc, conv_w, conv_b))
    xs = xbc[..., :SSD_INNER].reshape(Bsz, L, SSD_HEADS, SSD_HEAD_DIM).astype(jnp.float32)
    bm = xbc[..., SSD_INNER:SSD_INNER + gn].reshape(Bsz, L, SSD_GROUPS, SSD_STATE)
    cm = xbc[..., SSD_INNER + gn:].reshape(Bsz, L, SSD_GROUPS, SSD_STATE)
    dt = jax.nn.softplus(dt_raw.reshape(Bsz, L, 2, SSD_HEADS).astype(jnp.float32)
                         + dt_bias.astype(jnp.float32))
    a = -jnp.exp(a_log.astype(jnp.float32))
    flip = lambda t: jnp.flip(t, axis=1)
    y_fwd = _ssd_scan(xs * dt[:, :, 0, :, None], dt[:, :, 0] * a[0], bm, cm)
    y_bwd = flip(_ssd_scan(flip(xs * dt[:, :, 1, :, None]), flip(dt[:, :, 1] * a[1]),
                           flip(bm), flip(cm)))
    y = y_fwd + y_bwd + d_skip.astype(jnp.float32)[:, None] * xs
    y = y.reshape(Bsz, L, SSD_INNER) * jax.nn.silu(z.astype(jnp.float32))
    return _rmsnorm(y, norm_w)

def _diff_attention(q, k, v, lam):
    Bsz, S = q.shape[0], q.shape[1]
    nb = S // Q_BLOCK
    qb = jnp.moveaxis(q.reshape(Bsz, nb, Q_BLOCK, DIFF_HEADS, 2, DIFF_HEAD_DIM), 1, 0)
    vf = v.astype(jnp.float32)
    scale = DIFF_HEAD_DIM ** -0.5
    def block(qblk):
        s = jnp.einsum('bqhcd,bkhcd->bhcqk', qblk, k) * scale
        p = jax.nn.softmax(s.astype(jnp.float32), axis=-1)
        w = p[:, :, 0] - lam * p[:, :, 1]
        return jnp.einsum('bhqk,bkhe->bqhe', w, vf)
    o = lax.map(block, qb)
    return jnp.moveaxis(o, 0, 1).reshape(Bsz, S, DIFF_HEADS, 2 * DIFF_HEAD_DIM)

def _memory_cross_attention(q, mem_kv):
    mk, mv = mem_kv[:, :, 0], mem_kv[:, :, 1]
    s = jnp.einsum('bshd,bmhd->bhsm', q, mk).astype(jnp.float32) * (CROSS_HEAD_DIM ** -0.5)
    p = jax.nn.softmax(s, axis=-1)
    return jnp.einsum('bhsm,bmhd->bshd', p, mv.astype(jnp.float32))

def second_inputs(seed: int = 0) -> dict:
    key = jax.random.key(seed)
    ks = jax.random.split(key, 20)
    f32 = jnp.float32
    def nrm(k, shape, scale):
        return jax.random.normal(k, shape, f32) * scale
    x = nrm(ks[0], (BATCH, SEQ, D_MODEL), 1.0)
    mem = nrm(ks[1], (BATCH, MEM_TOKENS, D_MODEL), 1.0)
    offsets = jax.random.randint(ks[2], (BATCH, 1), 0, 4096, dtype=jnp.int32)
    positions = offsets + jnp.arange(SEQ, dtype=jnp.int32)[None, :]
    w_in = nrm(ks[3], (DEPTH, D_MODEL, IN_COLS), D_MODEL ** -0.5)
    conv_w = nrm(ks[4], (DEPTH, SSD_CONV, SSD_CONV_CH), SSD_CONV ** -0.5)
    conv_b = nrm(ks[5], (DEPTH, SSD_CONV_CH), 0.01)
    dt0 = jnp.exp(jax.random.uniform(ks[6], (DEPTH, 2, SSD_HEADS), f32,
                                     math.log(1e-3), math.log(1e-1)))
    dt_bias = dt0 + jnp.log(-jnp.expm1(-dt0))
    a_log = jnp.log(jax.random.uniform(ks[7], (DEPTH, 2, SSD_HEADS), f32, 1.0, 16.0))
    d_skip = 1.0 + nrm(ks[8], (DEPTH, SSD_HEADS), 0.01)
    ssd_norm_w = 1.0 + nrm(ks[9], (DEPTH, SSD_INNER), 0.01)
    diff_lam = nrm(ks[10], (DEPTH, 4, DIFF_HEAD_DIM), 0.1)
    diff_norm_w = 1.0 + nrm(ks[11], (DEPTH, 2 * DIFF_HEAD_DIM), 0.01)
    w_mem_kv = nrm(ks[12], (DEPTH, D_MODEL, 2 * CROSS_WIDTH), D_MODEL ** -0.5)
    w_br_ssd = nrm(ks[13], (DEPTH, SSD_INNER, D_MODEL), SSD_INNER ** -0.5 * DEEPNORM_BETA)
    w_br_diff = nrm(ks[14], (DEPTH, DIFF_WIDTH, D_MODEL), DIFF_WIDTH ** -0.5 * DEEPNORM_BETA)
    w_br_cross = nrm(ks[15], (DEPTH, CROSS_WIDTH, D_MODEL), CROSS_WIDTH ** -0.5 * DEEPNORM_BETA)
    gate_b = nrm(ks[16], (DEPTH, N_BRANCH, D_MODEL), 0.01)
    w_out = nrm(ks[17], (DEPTH, D_MODEL, D_MODEL), D_MODEL ** -0.5 * DEEPNORM_BETA)
    ln_g = 1.0 + nrm(ks[18], (DEPTH, D_MODEL), 0.01)
    ln_b = nrm(ks[19], (DEPTH, D_MODEL), 0.01)
    return {'x': x, 'mem': mem, 'positions': positions, 'w_in': w_in,
            'conv_w': conv_w, 'conv_b': conv_b, 'dt_bias': dt_bias, 'a_log': a_log,
            'd_skip': d_skip, 'ssd_norm_w': ssd_norm_w, 'diff_lam': diff_lam,
            'diff_norm_w': diff_norm_w, 'w_mem_kv': w_mem_kv, 'w_br_ssd': w_br_ssd,
            'w_br_diff': w_br_diff, 'w_br_cross': w_br_cross, 'gate_b': gate_b,
            'w_out': w_out, 'ln_g': ln_g, 'ln_b': ln_b}

def second_block(x, mem, positions, w_in, conv_w, conv_b, dt_bias, a_log, d_skip,
              ssd_norm_w, diff_lam, diff_norm_w, w_mem_kv, w_br_ssd, w_br_diff,
              w_br_cross, gate_b, w_out, ln_g, ln_b):
    Bsz, S, _ = x.shape
    cos, sin = _rope_tables(positions)
    splits = _in_splits()
    for layer in range(DEPTH):
        lambda_init = 0.8 - 0.6 * math.exp(-0.3 * layer)
        proj = jnp.einsum('bsd,de->bse', x, w_in[layer])
        z, xbc, dt_raw, dq, dk, dv, dg, cq, cg, gl = jnp.split(proj, splits, axis=-1)

        y_ssd = _ssd_branch(z, xbc, dt_raw, conv_w[layer], conv_b[layer], dt_bias[layer],
                            a_log[layer], d_skip[layer], ssd_norm_w[layer])

        lq = diff_lam[layer].astype(jnp.float32)
        lam = (jnp.exp(jnp.sum(lq[0] * lq[1])) - jnp.exp(jnp.sum(lq[2] * lq[3]))
               + lambda_init)
        q = _apply_rope(dq.reshape(Bsz, S, DIFF_HEADS, 2, DIFF_HEAD_DIM), cos, sin)
        k = _apply_rope(dk.reshape(Bsz, S, DIFF_HEADS, 2, DIFF_HEAD_DIM), cos, sin)
        v = dv.reshape(Bsz, S, DIFF_HEADS, 2 * DIFF_HEAD_DIM)
        o = _diff_attention(q, k, v, lam)
        o = _rmsnorm(o, diff_norm_w[layer]) * (1.0 - lambda_init)
        y_diff = o.reshape(Bsz, S, DIFF_WIDTH) * jax.nn.silu(dg.astype(jnp.float32))

        mem_kv = jnp.einsum('bmd,de->bme', mem, w_mem_kv[layer]).reshape(
            Bsz, MEM_TOKENS, 2, CROSS_HEADS, CROSS_HEAD_DIM)
        oc = _memory_cross_attention(cq.reshape(Bsz, S, CROSS_HEADS, CROSS_HEAD_DIM), mem_kv)
        y_cross = oc.reshape(Bsz, S, CROSS_WIDTH) * jax.nn.silu(cg.astype(jnp.float32))

        gates = jax.nn.sigmoid(gl.reshape(Bsz, S, N_BRANCH, D_MODEL).astype(jnp.float32)
                               + gate_b[layer].astype(jnp.float32))
        merged = (gates[:, :, 0] * jnp.einsum('bse,ed->bsd', y_ssd, w_br_ssd[layer])
                  + gates[:, :, 1] * jnp.einsum('bse,ed->bsd', y_diff, w_br_diff[layer])
                  + gates[:, :, 2] * jnp.einsum('bse,ed->bsd', y_cross, w_br_cross[layer]))
        out = jnp.einsum('bsd,de->bse', merged, w_out[layer])

        x = _layernorm(DEEPNORM_ALPHA * x.astype(jnp.float32) + out,
                       ln_g[layer], ln_b[layer]).astype(x.dtype)
    return x


def setup_inputs(seed=0):
    out = dict(first_inputs(seed))
    for name, value in second_inputs(seed + 1).items():
        if name != "x":
            out[name + "_2"] = value
    return out


def reference(
    x, c, positions, ada_w, ada_b, norm_mix, w_in, attn_q_norm, attn_k_norm, attn_sinks,
    hgrn_lb_logits, hgrn_out_norm, gdn_conv_w, gdn_a_log, gdn_dt_bias, gdn_out_norm, w_out,
    norm_ffn, w_gate, w_up, w_down, mem_2, positions_2, w_in_2, conv_w_2, conv_b_2, dt_bias_2,
    a_log_2, d_skip_2, ssd_norm_w_2, diff_lam_2, diff_norm_w_2, w_mem_kv_2, w_br_ssd_2,
    w_br_diff_2, w_br_cross_2, gate_b_2, w_out_2, ln_g_2, ln_b_2,
):
    x = first_block(
        x, c, positions, ada_w, ada_b, norm_mix, w_in, attn_q_norm, attn_k_norm, attn_sinks,
        hgrn_lb_logits, hgrn_out_norm, gdn_conv_w, gdn_a_log, gdn_dt_bias, gdn_out_norm, w_out,
        norm_ffn, w_gate, w_up, w_down,
    )
    return second_block(
        x, mem_2, positions_2, w_in_2, conv_w_2, conv_b_2, dt_bias_2, a_log_2, d_skip_2,
        ssd_norm_w_2, diff_lam_2, diff_norm_w_2, w_mem_kv_2, w_br_ssd_2, w_br_diff_2,
        w_br_cross_2, gate_b_2, w_out_2, ln_g_2, ln_b_2,
    )


_drawn_inputs = setup_inputs


def setup_inputs(seed=0):
    import zlib

    import numpy as np

    out = dict(_drawn_inputs(seed))
    spreads = {}
    factors = {'attn_q_norm': 8.0,
     'attn_k_norm': 8.0,
     'attn_sinks': 8.0,
     'hgrn_out_norm': 6.538,
     'gdn_out_norm': 8.0,
     'norm_ffn': 2.742,
     'mem_2': 6.445,
     'conv_b_2': 64.0,
     'd_skip_2': 200.0,
     'ssd_norm_w_2': 200.0,
     'diff_lam_2': 8.0,
     'diff_norm_w_2': 64.0,
     'w_mem_kv_2': 6.172,
     'w_br_cross_2': 6.148,
     'gate_b_2': 8.0,
     'ln_g_2': 3.986,
     'ln_b_2': 3.894}
    for name, (base, spread) in spreads.items():
        noise = np.random.default_rng([zlib.crc32(name.encode()), seed]).standard_normal(out[name].shape)
        drawn = base * np.exp(spread * noise) if base else spread * noise
        out[name] = __import__('jax').numpy.asarray(drawn.astype(out[name].dtype))
    for name, factor in factors.items():
        out[name] = (out[name] * factor).astype(out[name].dtype)
    return out
```

```python
import math
from contextlib import ExitStack

import concourse.bass as bass
from concourse import mybir

F32 = mybir.dt.float32
I32 = mybir.dt.int32
ALU = mybir.AluOpType
ACT = mybir.ActivationFunctionType
AX = mybir.AxisListType.X

D = 1024
S = 512
FF = 2816
N_IN1 = 2824
N_IN2 = 14400
ALPHA = 4.0 ** 0.25
TWO_PI = 2.0 * math.pi
RING = 4
KS = 4
ARENA = 30720

C1 = dict(nmix=0, nffn=8, adab=16, lb0=64, lb1=66, conv=68, gain=92)
NC1 = 96
C2 = dict(conv=0, cb=120, ssd=144, diff=160)
NC2 = 161
R1 = dict(qn=0, kn=64, sink=128, alog=136, dtb=140)
NR1 = 144
R2 = dict(dtb=0, alog=64, skip=128, lam=160)
NR2 = 416
K_ID, K_U, K_L, K_NF, K_NB, K_ONE, K_AM, K_LV = 0, 128, 256, 384, 512, 640, 768, 1024
K_F8, K_F32 = K_LV + 7 * 128, K_LV + 7 * 128 + 8
NK = K_F32 + 32


class Queue:

    def __init__(self, sem, chain):
        self.sem, self.chain, self.n, self.ops = sem, chain, 0, []

    def __call__(self, fn, *waits, inc=True):
        w = [t for t in waits if t is not None]
        if self.chain and self.n:
            w.append((self.sem, self.n))
        self.ops.append((w, fn, self.sem if inc else None, 1))
        if inc:
            self.n += 1
        return (self.sem, self.n)

    def now(self):
        return (self.sem, self.n) if self.n else None

    def emit(self, eng):
        seen = {}
        for waits, fn, sem, by in self.ops:
            for s, v in waits:
                if seen.get(s.name, 0) < v:
                    eng.wait_ge(s, v)
                    seen[s.name] = v
            ins = fn(eng) if fn else None
            if sem is not None:
                ins.then_inc(sem, by)


class Load:

    def __init__(self, sem):
        self.sem, self.n = sem, 0

    def start(self, q, out, in_, *waits):
        w = [t for t in waits if t is not None]
        if self.n:
            w.append((self.sem, self.n))
        q.ops.append((w, lambda e: e.dma_start(out, in_), self.sem, 16))
        self.n += 16
        return (self.sem, self.n)


class Bank:
    def __init__(self, ap):
        self.ap, self.free = ap, ()


def bc(ap, axis, n):
    v = ap.unsqueeze(axis)
    shape = list(v.shape)
    shape[axis] = n
    return v.to_broadcast(shape)


def program(nc, T, out):
    ctx = ExitStack()
    with ctx:
        def sb(name, shape, dt=F32):
            return ctx.enter_context(nc.sbuf_tensor(name, shape, dt))

        def sem(name):
            return ctx.enter_context(nc.semaphore(name))

        cst = sb("cst", [128, NK])
        X = sb("X", [128, 4, D])
        HT = sb("HT", [128, 8, S])
        RG = [sb(f"ring{i}", [128, KS, 512]) for i in range(RING)]
        AR = sb("arena", [128, ARENA])
        c1 = sb("c1", [128, NC1])
        r1 = sb("r1", [128, NR1])
        c2 = sb("c2", [128, NC2])
        r2 = sb("r2", [128, NR2])
        sm = sb("sm", [128, 640])
        tabs = sb("tabs", [128, 4, 80])
        pos = sb("pos", [128, 8], I32)
        Zd = nc.dram_tensor("zd", (4, 128, 2048), F32, kind="Internal").ap()
        Gd = nc.dram_tensor("gd", (4, 128, 3072), F32, kind="Internal").ap()
        Dg = nc.dram_tensor("dgd", (4, 128, 1024), F32, kind="Internal").ap()
        Cg = nc.dram_tensor("cgd", (4, 128, 1024), F32, kind="Internal").ap()
        GTd = nc.dram_tensor("gtd", (1, 2, 1024), F32, kind="Internal").ap()
        Xd = nc.dram_tensor("xd", (128, 4, 1024), F32, kind="Internal").ap()
        banks = [Bank(ctx.enter_context(nc.psum_tensor(f"ps{i}", [128, 512], F32))) for i in range(8)]

        PE = Queue(sem("s_pe"), False)
        V = Queue(sem("s_dve"), True)
        A = Queue(sem("s_act"), True)
        P = Queue(sem("s_pool"), True)
        SP = Queue(sem("s_sp"), False)

        s_misc = [Load(sem(f"s_misc{i}")) for i in range(12)]
        s_ring = [Load(sem(f"s_ring{i}")) for i in range(RING)]
        s_st = [Load(sem(f"s_st{i}")) for i in range(4)]

        ident = cst[:, K_ID:K_ID + 128]
        U = cst[:, K_U:K_U + 128]
        Lr = cst[:, K_L:K_L + 128]
        NF = cst[:, K_NF:K_NF + 128]
        NB = cst[:, K_NB:K_NB + 128]
        ones = cst[:, K_ONE:K_ONE + 128]
        AM = cst[:, K_AM:K_AM + 256]
        LV = [cst[:, K_LV + 128 * i:K_LV + 128 * (i + 1)] for i in range(7)]

        def ar(off, *shape):
            n = 1
            for s in shape:
                n *= s
            assert off + n <= ARENA, (off, n)
            v = AR[:, off:off + n]
            if len(shape) == 2:
                v = v.rearrange("p (a b) -> p a b", a=shape[0])
            elif len(shape) == 3:
                v = v.rearrange("p (a b c) -> p a b c", a=shape[0], b=shape[1])
            return v

        def tt(o, a, b, op, *w):
            return V(lambda e: e.tensor_tensor(o, a, b, op), *w)

        def ts(o, a, s1, s2, op0, op1=None, *w):
            if op1 is None:
                return V(lambda e: e.tensor_scalar(o, a, s1, None, op0), *w)
            return V(lambda e: e.tensor_scalar(o, a, s1, s2, op0, op1), *w)

        def stt(o, a, s1, b, op0, op1, *w):
            return V(lambda e: e.scalar_tensor_tensor(out=o, in0=a, scalar=s1, in1=b, op0=op0, op1=op1), *w)

        def red(o, a, op, *w):
            return V(lambda e: e.tensor_reduce(o, a, AX, op), *w)

        def rec(o, a, *w):
            return V(lambda e: e.reciprocal(o, a), *w)

        def vcp(o, a, *w):
            return V(lambda e: e.tensor_copy(o, a), *w)

        def act(o, a, f, *w, scale=1.0, bias=None, acc=None):
            kw = dict(scale=scale)
            if bias is not None:
                kw["bias"] = bias
            if acc is not None:
                kw["accum_out"] = acc
            return A(lambda e: e.activation(o, a, f, **kw), *w)

        def acp(o, a, *w):
            return act(o, a, ACT.Copy, *w)

        def take():
            assert banks, "every bank is held"
            return banks.pop(0)

        def give(b, *tokens):
            b.free = tokens
            banks.append(b)

        def mm(o, pairs, *w):
            for i, (l, r) in enumerate(pairs):
                st, sp = i == 0, i == len(pairs) - 1
                t = PE(lambda e, l=l, r=r, st=st, sp=sp: e.matmul(o, l, r, start=st, stop=sp),
                       *(w if st else ()), inc=sp)
            return t

        def tr(o, i, *w):
            return PE(lambda e: e.transpose(o, i, ident), *w)

        def rstd(buf, n, scale, eps):
            a = ts(buf, buf, scale, eps, ALU.mult, ALU.add)
            b = act(buf, buf, ACT.Sqrt, a)
            return rec(buf, buf, b)

        HO = (0, 2, 1, 3)

        def rowsw(h):
            return PE.now() if h == 1 else None

        sides = []

        def pump():
            while sides:
                try:
                    next(sides[0])
                    return
                except StopIteration:
                    sides.pop(0)

        def drain():
            while sides:
                pump()

        slot_free = [()] * RING
        n_slot = [0]

        def wload(src, kk, nw):
            i = n_slot[0] % RING
            n_slot[0] += 1
            v = RG[i][:, 0:kk, 0:nw]
            t = s_ring[i].start(SP, v, src, *slot_free[i])
            return i, v, t

        def gemm_t(w, n0, nw, kt, lhs, need, evict, nm=4):
            held = [None] * 4
            for k0 in range(0, kt, KS):
                kk = min(KS, kt - k0)
                i, v, t = wload(w[k0 * 128:(k0 + kk) * 128, n0:n0 + nw].rearrange("(k p) n -> p k n", p=128), kk, nw)
                for m in range(nm):
                    if k0 == 0:
                        held[m] = take()
                    b = held[m]
                    for k in range(kk):
                        first, last = k0 + k == 0, k0 + k == kt - 1
                        wt = (*b.free, *need, t) if k == 0 else ()
                        if k0 and k == 0:
                            wt = (t, *need)
                        tok = PE(lambda e, b=b, k=k, m=m, k0=k0, v=v, first=first, last=last: e.matmul(
                            b.ap[:, 0:nw], lhs[:, k0 + k, m * 128:(m + 1) * 128], v[:, k, :],
                            start=first, stop=last), *wt, inc=(k == kk - 1))
                    if k0 + kk == kt:
                        give(b, *evict(m, b.ap[:, 0:nw], tok))
                    pump()
                slot_free[i] = (tok,)

        def gemm_c(w, n0, nw, rhs, ns, need, evict):
            held = [None] * 4
            for k0 in range(0, 8, KS):
                i, v, t = wload(w[k0 * 128:(k0 + KS) * 128, n0:n0 + nw].rearrange("(k p) n -> p k n", p=128), KS, nw)
                for c in range(nw // 128):
                    if k0 == 0:
                        held[c] = take()
                    b = held[c]
                    for k in range(KS):
                        wt = (*b.free, *need, t) if k0 == 0 else (t,)
                        tok = PE(lambda e, b=b, k=k, c=c, v=v, k0=k0: e.matmul(
                            b.ap[:, 0:ns], v[:, k, c * 128:(c + 1) * 128], rhs[:, k0 + k, 0:ns],
                            start=(k0 + k == 0), stop=(k0 + k == 7)), *(wt if k == 0 else ()), inc=(k == KS - 1))
                    if k0 + KS == 8:
                        give(b, *evict(c, b.ap[:, 0:ns], tok))
                    pump()
                slot_free[i] = (tok,)

        def fence():
            return [q.now() for q in (PE, V, A)]

        def join(*extra):
            f = [x for x in fence() if x] + [x for x in extra if x]
            for q in (PE, V, A):
                q.ops.append((f, None, None, 0))

        t_cst = s_misc[0].start(SP, cst[:, :], T["cst"])
        t_pos = s_misc[1].start(SP, pos[:, :], T["pos"])
        t_x = s_misc[2].start(SP, X[:, :, :], T["x"].rearrange("o (m p) d -> p (o m) d", p=128))
        cc = sm[:, 0:8]
        t_c = s_misc[3].start(SP, cc, T["c"])
        join(t_cst, t_pos, t_x, t_c)
        cond = sm[:, 8:16]
        t = act(cond, cc, ACT.Tanh, scale=0.5)
        t = stt(cond, cond, 1.0, cc, ALU.add, ALU.mult, t)
        ts(cond, cond, 0.5, None, ALU.mult)

        MAGIC = 12582912.0
        C_A, C_B = 6.28125, 0.0019340515136718750
        C_C = TWO_PI - C_A - C_B
        pf = sm[:, 16:24]
        vcp(pf, pos[:, :])
        for which, (n, o, kf) in enumerate(((8, 0, K_F8), (32, 16, K_F32))):
            for m in range(4):
                ang = sm[:, 32:32 + n]
                rn = sm[:, 64:64 + n]
                ts(ang, cst[:, kf:kf + n], pf[:, 4 * which + m:4 * which + m + 1], None, ALU.mult)
                for cos in (1, 0):
                    dst = tabs[:, m, o + (0 if cos else n):o + (0 if cos else n) + n]
                    ts(rn, ang, 1.0 / TWO_PI, 0.25 * cos, ALU.mult, ALU.add)
                    ts(rn, rn, MAGIC, None, ALU.add)
                    ts(rn, rn, -MAGIC, None, ALU.add)
                    stt(dst, rn, -C_A, ang, ALU.mult, ALU.add)
                    stt(dst, rn, -C_B, dst, ALU.mult, ALU.add)
                    stt(dst, rn, -C_C, dst, ALU.mult, ALU.add)
                    ts(dst, dst, math.pi / 2 * cos, None, ALU.add)
                    ts(dst, dst, 3.1415925, -3.1415925, ALU.min, ALU.max)
        t = V.now()
        for m in range(4):
            act(tabs[:, m, :], tabs[:, m, :], ACT.Sin, t)

        def norm_stats(src, eps):
            j = ar(ARENA - 1024, 1024)
            for m in range(4):
                act(j, src[:, m, :], ACT.Square, V.now(), acc=sm[:, 600 + m:601 + m])
            a = ts(sm[:, 600:604], sm[:, 600:604], 1.0 / D, eps, ALU.mult, ALU.add, A.now())
            b = act(sm[:, 600:604], sm[:, 600:604], ACT.Sqrt, a)
            rec(sm[:, 600:604], sm[:, 600:604], b)

        def to_ht(src, scale, bias, *w, dst=HT, nk=8, m0=0):
            for k in range(nk):
                b = take()
                for m in range(4):
                    t = tr(b.ap[:, m * 128:(m + 1) * 128], src[:, m, k * 128:(k + 1) * 128],
                           *(b.free if m == 0 else ()), *w)
                if scale is None:
                    t = acp(dst[:, k, :], b.ap[:, :], t) if k % 2 else vcp(dst[:, k, :], b.ap[:, :], t)
                elif bias is None:
                    sc = scale[:, k:k + 1]
                    t = ts(dst[:, k, :], b.ap[:, :], sc, None, ALU.mult, None, t) if k % 2 else \
                        act(dst[:, k, :], b.ap[:, :], ACT.Copy, t, scale=sc)
                elif k % 2:
                    t = ts(dst[:, k, :], b.ap[:, :], scale[:, k:k + 1], bias[:, k:k + 1], ALU.mult, ALU.add, t)
                else:
                    t = act(dst[:, k, :], b.ap[:, :], ACT.Identity, t, scale=scale[:, k:k + 1], bias=bias[:, k:k + 1])
                give(b, t)
            return (V.now(), A.now())

        O_ATT, O_HG, O_C = 0, 7680, 7680 + 9344
        O_MIX = O_C + 3090 + 3072 + 1024 + 6
        mods = sm[:, 24:24 + 48]

        def first(l):
            t1 = s_misc[4].start(P, c1[:, :], T["c1"][l], V.now(), A.now())
            t2 = s_misc[5].start(P, r1[:, :], T["r1"][l].partition_broadcast(128), V.now(), A.now())
            GT = ar(0, 2, 1024)
            accs = [ar(2048 + 512 * i, 512) for i in range(2)]
            t3 = s_misc[6].start(P, GT, T["gtb"][l].rearrange("(a n) -> a n", a=2).partition_broadcast(128),
                                 PE.now(), V.now(), A.now())
            join(t1, t2, t3)
            pend = [None, None]
            for nb in range(12):
                acc = accs[nb % 2]
                for k0 in range(0, 8, KS):
                    i, v, t = wload(T["ada_w"][l][k0 * 128:(k0 + KS) * 128, nb * 512:(nb + 1) * 512].rearrange(
                        "(k p) n -> p k n", p=128), KS, 512)
                    for k in range(k0, k0 + KS):
                        if k == 0:
                            tv = ts(acc, v[:, 0, :], cond[:, 0:1], None, ALU.mult, None, t, pend[nb % 2])
                        else:
                            tv = stt(acc, v[:, k - k0, :], cond[:, k:k + 1], acc, ALU.mult, ALU.add, t)
                    slot_free[i] = (tv,)
                part = nb // 2
                b = take()
                if part in (2, 5):
                    tp = mm(b.ap[:, :], [(ones, acc)], tv, *b.free)
                    g = GT[:, part // 3, (nb % 2) * 512:(nb % 2) * 512 + 512]
                    te = tt(g, b.ap[:, :], g, ALU.add, tp)
                else:
                    for j in range(4):
                        tp = mm(b.ap[:, j:j + 1], [(acc[:, j * 128:(j + 1) * 128], ones[:, 0:1])], tv, *b.free)
                    te = tt(mods[:, nb * 4:nb * 4 + 4], b.ap[:, 0:4],
                            c1[:, C1["adab"] + nb * 4:C1["adab"] + nb * 4 + 4], ALU.add, tp)
                pend[nb % 2] = tp
                give(b, te)
            t_gt = s_st[2].start(P, GTd, GT[0:1, :, :], te)
            for part, gain in ((1, "nmix"), (4, "nffn")):
                md = mods[:, part * 8:part * 8 + 8]
                stt(md, md, 1.0, c1[:, C1[gain]:C1[gain] + 8], ALU.add, ALU.mult)
            join(t_gt)
            norm_stats(X, 1e-6)
            xn = ar(0, 4, 1024)
            for m in range(4):
                ts(xn[:, m, :], X[:, m, :], sm[:, 600 + m:601 + m], None, ALU.mult)
            need = to_ht(xn, mods[:, 8:16], mods[:, 0:8], V.now())
            join()
            W = T["w_in"][l]
            MIX = ar(O_MIX, 8, 512)

            QK = ar(O_ATT, 4, 640)
            QKT = ar(O_ATT + 2560, 5, 512)
            AV = ar(O_ATT + 5120, 4, 128)
            PT = ar(O_ATT + 5632, 4, 512)
            BQ, Zb, BV, BG, KT, E_, XL = [ar(O_HG + 1024 * i, 1024) for i in range(7)]
            ACC = ar(O_HG + 7168, 4, 512)
            ST = ar(O_HG + 9216, 2, 64)
            BQ3, Z3, KT3 = [z.rearrange("p (a b) -> p a b", a=2) for z in (BQ, Zb, KT)]
            BV3, BG3 = [z.rearrange("p (a b) -> p a b", a=4) for z in (BV, BG)]
            CIN = ar(O_C, 6, 515)
            CT = ar(O_C + 3096, 6, 512)
            CG = ar(O_C + 3096 + 3072, 4, 256)
            CBA = sm[:, 80:112].rearrange("p (a b) -> p a b", a=4)

            def ev0(m, p, t):
                o = QK[:, m, 0:512].rearrange("p (i j d) -> p j i d", i=4, j=2)
                return (vcp(o, p.rearrange("p (j i d) -> p j i d", j=2, i=4), t),)

            def ev1(m, p, t):
                acp(QK[:, m, 512:640], p[:, 0:128], t)
                return (acp(AV[:, m, :], p[:, 128:256], t),)

            def ev2(c, p, t):
                return (acp((BQ3, Z3)[c // 2][:, c % 2, :], p, t),)

            def ev3(m, p, t):
                acp(BV3[:, m, :], p[:, 0:256], t)
                return (acp(BG3[:, m, :], p[:, 256:512], t),)

            def ev_c(c0):
                def ev(c, p, t):
                    return (acp(CIN[:, c0 + c, 3:515], p, t),)
                return ev

            def ev6(m, p, t):
                acp(CG[:, m, :], p[:, 0:256], t)
                return (acp(CBA[:, m, :], p[:, 256:264], t),)

            def attention():
                join()
                sq = PT.rearrange("p a b -> p (a b)")[:, 0:640]
                ss = sm[:, 120:160]
                for m in range(4):
                    tt(sq, QK[:, m, :], QK[:, m, :], ALU.mult)
                    red(ss[:, m * 10:m * 10 + 10], sq.rearrange("p (h d) -> p h d", d=64), ALU.add)
                rstd(ss, 40, 1.0 / 64, 1e-6)
                rt = [sm[:, 160 + 80 * i:240 + 80 * i].rearrange("p (h d) -> p h d", d=8) for i in range(4)]
                for m in range(4):
                    q = QK[:, m, :].rearrange("p (h d) -> p h d", d=64)
                    tt(q, q, bc(ss[:, m * 10:m * 10 + 10], 2, 64), ALU.mult)
                    tt(q[:, 0:8, :], q[:, 0:8, :], bc(r1[:, R1["qn"]:R1["qn"] + 64], 1, 8), ALU.mult)
                    tt(q[:, 8:10, :], q[:, 8:10, :], bc(r1[:, R1["kn"]:R1["kn"] + 64], 1, 2), ALU.mult)
                    cs, sn = bc(tabs[:, m, 0:8], 1, 10), bc(tabs[:, m, 8:16], 1, 10)
                    x1, x2 = q[:, :, 0:8], q[:, :, 8:16]
                    tt(rt[0], x1, cs, ALU.mult)
                    tt(rt[1], x2, sn, ALU.mult)
                    tt(rt[2], x2, cs, ALU.mult)
                    tt(rt[3], x1, sn, ALU.mult)
                    tt(x1, rt[0], rt[1], ALU.subtract)
                    t = tt(x2, rt[2], rt[3], ALU.add)
                    yield
                for i in range(5):
                    b = take()
                    for m in range(4):
                        tp = tr(b.ap[:, m * 128:(m + 1) * 128], QK[:, m, i * 128:(i + 1) * 128],
                                t, *(b.free if m == 0 else ()))
                    te = acp(QKT[:, i, :], b.ap[:, :], tp)
                    give(b, te)
                yield
                SC = ar(O_ATT, 8, 256)
                t_read = tp
                for m in range(4):
                    kw = 128 if m == 0 else 256
                    k0 = max(0, m - 1) * 128
                    am = AM[:, 256 - kw:256]
                    for g in range(4):
                        b = take()
                        for u in range(2):
                            j, i = divmod(2 * g + u, 4)
                            tp = mm(b.ap[:, u * 256:u * 256 + kw],
                                    [(QKT[j * 64:j * 64 + 64, i, m * 128:(m + 1) * 128],
                                      QKT[j * 64:j * 64 + 64, 4, k0:k0 + kw])], te, *b.free)
                        tv = stt(SC[:, 2 * g:2 * g + 2, 0:kw],
                                 b.ap.rearrange("p (u k) -> p u k", u=2)[:, :, 0:kw], 0.125,
                                 bc(am, 1, 2), ALU.mult, ALU.add, tp, t_read)
                        give(b, tv)
                    mx, su, es = sm[:, 480:488], sm[:, 488:496], sm[:, 496:504]
                    sink = r1[:, R1["sink"]:R1["sink"] + 8]
                    s = SC[:, :, 0:kw]
                    red(mx, s, ALU.max)
                    tt(mx, mx, sink, ALU.max)
                    tt(es, sink, mx, ALU.subtract)
                    tv = tt(s, s, bc(mx, 2, kw), ALU.subtract)
                    ta = act(es, es, ACT.Exp, tv)
                    ta = act(s, s, ACT.Exp, tv)
                    yield
                    red(su, s, ALU.add, ta)
                    tt(su, su, es, ALU.add)
                    rec(su, su)
                    tv = tt(s, s, bc(su, 2, kw), ALU.mult)
                    yield
                    nk = kw // 128
                    for kt in range(nk):
                        for j in range(2):
                            b = take()
                            for i in range(4):
                                tp = tr(b.ap[:, i * 128:(i + 1) * 128],
                                        SC[:, j * 4 + i, kt * 128:(kt + 1) * 128], tv, *b.free)
                            te2 = acp(PT[:, kt * 2 + j, :], b.ap[:, :], tp, t_pv if m else None)
                            give(b, te2)
                    t_read = tp
                    yield
                    b = take()
                    for j in range(2):
                        tp = mm(b.ap[j * 64:j * 64 + 64, :],
                                [(AV[:, k0 // 128 + kt, j * 64:j * 64 + 64], PT[:, kt * 2 + j, :]) for kt in range(nk)],
                                te2, *b.free)
                    t_pv = tp
                    te2 = vcp(MIX[:, 0:4, m * 128:(m + 1) * 128], b.ap.rearrange("p (i q) -> p i q", i=4), tp)
                    give(b, te2)
                    yield

            def finish(o, gate, tile0):
                sq = E_.rearrange("p (a b) -> p a b", a=4)
                ss = sm[:, 512:528]
                tt(sq, o, o, ALU.mult)
                red(ss, E_.rearrange("p (h d) -> p h d", d=64), ALU.add)
                rstd(ss, 16, 1.0 / 64, 1e-6)
                for m in range(4):
                    q = o[:, m, :].rearrange("p (h d) -> p h d", d=64)
                    tt(q, q, bc(ss[:, 4 * m:4 * m + 4], 2, 64), ALU.mult)
                t = act(sq, gate, ACT.Tanh, V.now(), scale=0.5)
                stt(sq, sq, 1.0, gate, ALU.add, ALU.mult, t)
                t = stt(o, sq, 0.5, o, ALU.mult, ALU.mult)
                yield
                for k in range(2):
                    b = take()
                    for m in range(4):
                        tp = tr(b.ap[:, m * 128:(m + 1) * 128], o[:, m, k * 128:(k + 1) * 128], t, *b.free)
                    g = C1["gain"] + tile0 - 4 + k
                    te = ts(MIX[:, tile0 + k, :], b.ap[:, :], c1[:, g:g + 1], None, ALU.mult, None, tp)
                    give(b, te)
                yield

            def hgrn():
                join()
                U_, AZ, LU = E_, XL, ACC.rearrange("p a b -> p (a b)")[:, 0:1024]
                W_ = ACC.rearrange("p a b -> p (a b)")[:, 1024:2048]
                act(AZ, Zb, ACT.Abs, V.now())
                act(U_, AZ, ACT.Exp, scale=-1.0)
                t = act(LU, U_, ACT.Ln, bias=1.0)
                ts(W_, U_, 1.0, None, ALU.add, None, t)
                rec(W_, W_)
                stt(KT, Zb, 0.0, U_, ALU.is_lt, ALU.max)
                tt(KT, KT, W_, ALU.mult)
                if l == 0:
                    stt(Zb, Zb, 0.0, LU, ALU.min, ALU.subtract)
                else:
                    l0, l1 = c1[:, C1["lb0"]:C1["lb0"] + 2], c1[:, C1["lb1"]:C1["lb1"] + 2]
                    mx, e0, e1, sm2, lb, om = [sm[:, 530 + 2 * i:532 + 2 * i] for i in range(6)]
                    tt(mx, l0, l1, ALU.max)
                    tt(e0, l0, mx, ALU.subtract)
                    t = tt(e1, l1, mx, ALU.subtract)
                    act(e0, e0, ACT.Exp, t)
                    t = act(e1, e1, ACT.Exp)
                    tt(sm2, e0, e1, ALU.add, t)
                    rec(sm2, sm2)
                    tt(e0, e0, sm2, ALU.mult)
                    tt(e1, e1, sm2, ALU.mult)
                    tt(lb, e0, e1, ALU.add)
                    tt(lb, lb, e0, ALU.subtract)
                    ts(om, lb, -1.0, 1.0, ALU.mult, ALU.add)
                    ts(W_, U_, -1.0, 1.0, ALU.mult, ALU.add)
                    stt(W_, Zb, 0.0, W_, ALU.is_ge, ALU.mult)
                    for i in range(2):
                        h = slice(512 * i, 512 * i + 512)
                        ts(KT[:, h], KT[:, h], om[:, i:i + 1], None, ALU.mult)
                        t = stt(U_[:, h], W_[:, h], om[:, i:i + 1], U_[:, h], ALU.mult, ALU.add)
                        t = act(U_[:, h], U_[:, h], ACT.Ln, t, bias=lb[:, i:i + 1])
                        tt(Zb[:, h], U_[:, h], LU[:, h], ALU.subtract, t)
                yield
                for i in range(8):
                    s = slice(128 * i, 128 * i + 128)
                    V(lambda e, s=s: e.tensor_tensor_scan(XL[:, s], ones, Zb[:, s], 0.0, ALU.mult, ALU.add))
                vcp(Zb, XL)
                CUM = Zb
                yield
                tk = V.now()
                for c in range(4):
                    b = take()
                    for h in HO:
                        pr, ti = (h % 2) * 64, h // 2
                        tp = mm(b.ap[:, h * 128:(h + 1) * 128],
                                [(KT3[pr:pr + 64, ti, c * 128:(c + 1) * 128], BQ3[pr:pr + 64, ti, c * 128:(c + 1) * 128])],
                                tk, rowsw(h), *b.free)
                    te = tt(ACC[:, c, :].rearrange("p (h t) -> p h t", h=4),
                            b.ap.rearrange("p (h t) -> p h t", h=4), bc(ident, 1, 4), ALU.mult, tp)
                    give(b, te)
                yield
                for lv in range(7):
                    hb = 1 << lv

                    def halves(z):
                        v = z.rearrange("p (n u b) -> p n u b", u=2, b=hb)
                        return v[:, :, 0, :], v[:, :, 1, :]
                    cf, cs = halves(CUM)
                    ef, es = halves(E_)
                    xf, xs = halves(XL)
                    qf, qs = halves(BQ)
                    kf, ks = halves(KT)
                    ref = cf[:, :, hb - 1:hb].to_broadcast([128, 512 // hb, hb])
                    tt(es, cs, ref, ALU.subtract)
                    t = tt(ef, ref, cf, ALU.subtract)
                    t = act(E_, E_, ACT.Exp, t)
                    tt(xs, qs, es, ALU.mult, t, tp)
                    tx = tt(xf, kf, ef, ALU.mult)
                    yield
                    X3 = XL.rearrange("p (a b) -> p a b", a=2)
                    mk = bc(LV[lv], 1, 4).bitcast(I32)
                    for c in range(4):
                        b = take()
                        for h in HO:
                            pr, ti = (h % 2) * 64, h // 2
                            x = X3[pr:pr + 64, ti, c * 128:(c + 1) * 128]
                            tp = mm(b.ap[:, h * 128:(h + 1) * 128], [(x, x)], tx, rowsw(h), *b.free)
                        te = V(lambda e, c=c, b=b, mk=mk: e.copy_predicated(
                            ACC[:, c, :].rearrange("p (h t) -> p h t", h=4), mk,
                            b.ap.rearrange("p (h t) -> p h t", h=4)), tp)
                        give(b, te)
                        if c % 2:
                            yield
                last = CUM.rearrange("p (n t) -> p n t", t=128)[:, :, 127:128]
                C8 = CUM.rearrange("p (n t) -> p n t", t=128)
                EL = sm[:, 544:552]
                t = act(E_, CUM, ACT.Exp, V.now())
                tt(BQ, BQ, E_, ALU.mult, t, tp)
                t1 = act(EL, last.rearrange("p n o -> p (n o)"), ACT.Exp)
                t = tt(E_.rearrange("p (n t) -> p n t", t=128), last.to_broadcast([128, 8, 128]), C8, ALU.subtract, t1)
                t = act(E_, E_, ACT.Exp, t)
                t = tt(KT, KT, E_, ALU.mult, t)
                V(lambda e: e.memset(ST, 0.0))
                yield
                KD = E_.rearrange("p (a b) -> p a b", a=4)
                for m in range(0, 4, 2):
                    b = take()
                    for u in range(4):
                        tp = tr(b.ap[:, u * 128:(u + 1) * 128],
                                KT3[:, u % 2, (m + u // 2) * 128:(m + u // 2) * 128 + 128], t, *b.free)
                    te = vcp(KD[:, m:m + 2, :], b.ap.rearrange("p (a b) -> p a b", a=2), tp)
                    give(b, te)
                yield
                OB = XL.rearrange("p (a b) -> p a b", a=4)
                for c in range(4):
                    b, b2 = take(), take()
                    ts_ = V.now()
                    for h in range(4):
                        hs = slice(64 * h, 64 * h + 64)
                        tp = mm(b.ap[:, hs], [(ACC[:, c, h * 128:(h + 1) * 128], BV3[:, c, hs])], ts_, *b.free)
                    for h in HO:
                        pr, ti = (h % 2) * 64, h // 2
                        tp = mm(b.ap[:, 256 + 64 * h:320 + 64 * h],
                                [(BQ3[pr:pr + 64, ti, c * 128:(c + 1) * 128], ST[pr:pr + 64, ti, :])], rowsw(h))
                    for h in range(4):
                        pr, ti = (h % 2) * 64, h // 2
                        hs = slice(64 * h, 64 * h + 64)
                        tq = mm(b2.ap[pr:pr + 64, ti * 64:ti * 64 + 64], [(KD[:, c, hs], BV3[:, c, hs])], *b2.free)
                    vcp(OB[:, c, :], b.ap[:, 0:256], tp)
                    te = tt(OB[:, c, :], OB[:, c, :], b.ap[:, 256:512], ALU.add)
                    give(b, te)
                    for ti in range(2):
                        te = stt(ST[:, ti, :], ST[:, ti, :], EL[:, 4 * ti + c:4 * ti + c + 1],
                                 b2.ap[:, ti * 64:ti * 64 + 64], ALU.mult, ALU.add, tq)
                    give(b2, te)
                    yield
                yield from finish(OB, BG3, 4)

            def gdn():
                join()
                hw = sm[:, 560:584]
                ts(hw, c1[:, C1["conv"]:C1["conv"] + 24], 0.5, None, ALU.mult)
                TA = ar(O_ATT, 3072)
                for i in range(6):
                    t = V.now()
                    ts(CT[:, i, :], CIN[:, i, 0:512], hw[:, 4 * i:4 * i + 1], None, ALU.mult)
                    for j in range(1, 4):
                        t = stt(CT[:, i, :], CIN[:, i, j:j + 512], hw[:, 4 * i + j:4 * i + j + 1], CT[:, i, :],
                                ALU.mult, ALU.add)
                    th = TA[:, (i % 2) * 512:(i % 2) * 512 + 512]
                    t = act(th, CT[:, i, :], ACT.Tanh, t)
                    tc = stt(CT[:, i, :], th, 1.0, CT[:, i, :], ALU.add, ALU.mult, t)
                    if i % 2:
                        yield
                TOK = ar(O_ATT, 4, 768)
                for i in range(6):
                    b = take()
                    for m in range(4):
                        tp = tr(b.ap[:, m * 128:(m + 1) * 128], CT[:, i, m * 128:(m + 1) * 128], tc, *b.free)
                    te = acp(TOK[:, :, i * 128:(i + 1) * 128], b.ap.rearrange("p (m c) -> p m c", m=4), tp)
                    give(b, te)
                yield
                tct = tp
                be, g, gx, gu = [sm[:, 120 + 16 * i:136 + 16 * i] for i in range(4)]
                v3 = lambda z: z.rearrange("p (m h) -> p m h", m=4)
                t = act(v3(be), CBA[:, :, 0:4], ACT.Tanh, te, scale=0.5)
                ts(be, be, 1.0, 0.5, ALU.add, ALU.mult, t)
                t = tt(v3(g), CBA[:, :, 4:8], bc(r1[:, R1["dtb"]:R1["dtb"] + 4], 1, 4), ALU.add)
                act(gu, g, ACT.Abs, t)
                act(gu, gu, ACT.Exp, scale=-1.0)
                t = act(gx[:, 0:4], r1[:, R1["alog"]:R1["alog"] + 4], ACT.Exp)
                t = act(gu, gu, ACT.Ln, bias=1.0)
                stt(g, g, 0.0, gu, ALU.max, ALU.add, t)
                tg = stt(v3(g), v3(g), -1.0, bc(gx[:, 0:4], 1, 4), ALU.mult, ALU.mult)
                yield
                Gc, Gl, eG, eL, eD = [sm[:, 184 + 16 * i:200 + 16 * i] for i in range(5)]
                b = take()
                for m in range(4):
                    mm(b.ap[:, m * 4:m * 4 + 4], [(U, v3(g)[:, m, :])], tg, *b.free)
                    tp = mm(b.ap[:, 16 + m * 4:20 + m * 4], [(ones, v3(g)[:, m, :])])
                vcp(Gc, b.ap[:, 0:16], tp)
                te = vcp(Gl, b.ap[:, 16:32])
                give(b, te)
                t = tt(eD, Gl, Gc, ALU.subtract)
                act(eG, Gc, ACT.Exp, t)
                act(eL, Gl, ACT.Exp)
                tx = act(eD, eD, ACT.Exp)
                G5 = ar(O_ATT + 3072, 4, 512)
                GB = ar(O_HG + 4096, 2048)
                for m in range(4):
                    vcp(GB[:, 512 * m:512 * m + 512].rearrange("p (h s) -> p h s", h=4), bc(v3(g)[:, m, :], 2, 128))
                tb = V.now()
                yield
                for m in range(4):
                    b = take()
                    for h in range(4):
                        tp = mm(b.ap[:, h * 128:(h + 1) * 128], [(GB[:, 512 * m + 128 * h:512 * m + 128 * h + 128], U)],
                                tb, *b.free)
                    for h in range(4):
                        te = ts(G5[:, m, h * 128:(h + 1) * 128], b.ap[:, h * 128:(h + 1) * 128],
                                Gc[:, 4 * m + h:4 * m + h + 1], 0.0, ALU.subtract, ALU.min, tp)
                    give(b, te)
                yield
                ta = act(G5, G5, ACT.Exp, te)
                for m in range(4):
                    u = G5[:, m, :].rearrange("p (h t) -> p h t", h=4)
                    tt(u, u, bc(U, 1, 4), ALU.mult, ta)
                yield
                ss = sm[:, 264:296]
                sq = ar(O_HG + 4096, 512)
                for m in range(4):
                    tt(sq, TOK[:, m, 0:512], TOK[:, m, 0:512], ALU.mult, tx, tp)
                    red(ss[:, 8 * m:8 * m + 8], sq.rearrange("p (h d) -> p h d", d=64), ALU.add)
                rstd(ss, 32, 1.0, 1e-6)
                s3 = ss.rearrange("p (m h) -> p m h", m=4)
                ts(s3[:, :, 0:4], s3[:, :, 0:4], 0.125, None, ALU.mult)
                KB, QD, KG = [ar(O_C + 3096 + 1024 * i, 4, 256) for i in range(3)]
                for m in range(4):
                    qk = TOK[:, m, 0:512].rearrange("p (h d) -> p h d", d=64)
                    tt(qk, qk, bc(ss[:, 8 * m:8 * m + 8], 2, 64), ALU.mult, tct)
                    hd = lambda z: z.rearrange("p (h d) -> p h d", d=64)
                    q, k, v = [hd(TOK[:, m, 256 * i:256 * i + 256]) for i in range(3)]
                    sl = slice(4 * m, 4 * m + 4)
                    tt(hd(KB[:, m, :]), k, bc(be[:, sl], 2, 64), ALU.mult)
                    tt(hd(QD[:, m, :]), q, bc(eG[:, sl], 2, 64), ALU.mult)
                    tt(hd(KG[:, m, :]), hd(KB[:, m, :]), bc(eG[:, sl], 2, 64), ALU.mult)
                    tt(v, v, bc(be[:, sl], 2, 64), ALU.mult)
                t = V.now()
                yield
                TR = ar(O_HG, 4, 8, 128)
                for m in range(4):
                    for half in range(2):
                        b = take()
                        for u in range(4):
                            src = ((TOK[:, m, 0:256], TOK[:, m, 256:512]), (KB[:, m, :], QD[:, m, :]))[half][u // 2]
                            tp = tr(b.ap[:, u * 128:(u + 1) * 128], src[:, (u % 2) * 128:(u % 2) * 128 + 128], t, *b.free)
                        te = acp(TR[:, m, 4 * half:4 * half + 4, :], b.ap.rearrange("p (a b) -> p a b", a=4), tp)
                        give(b, te)
                yield
                for m in range(4):
                    k = TOK[:, m, 256:512].rearrange("p (h d) -> p h d", d=64)
                    tt(k, k, bc(eD[:, 4 * m:4 * m + 4], 2, 64), ALU.mult, tp)
                AT = ar(O_ATT + 5120, 4, 512)
                TT = ar(O_HG + 5120, 4, 512)
                TM = ar(O_C, 4, 512)
                XM = ar(O_C + 2048, 2, 512)
                for m in range(4):
                    for which in range(2):
                        b = take()
                        for h in HO:
                            pr, ti = (h % 2) * 64, h // 2
                            tp = mm(b.ap[:, h * 128:(h + 1) * 128],
                                    [(TR[pr:pr + 64, m, 2 + ti, :], TR[pr:pr + 64, m, (4 if which == 0 else 0) + ti, :])],
                                    te, rowsw(h), *b.free)
                        dst = AT if which == 0 else G5
                        te2 = tt(dst[:, m, :], b.ap[:, :], G5[:, m, :], ALU.mult, tp)
                        give(b, te2)
                    yield
                MA = ar(O_HG + 7168, 2, 512)
                tb_ = []
                for m in range(4):
                    a4, t4 = [z[:, m, :].rearrange("p (h t) -> p h t", h=4) for z in (AT, TT)]
                    stt(t4, a4, -1.0, bc(LV[0], 1, 4), ALU.mult, ALU.mult)
                    t = tt(t4, t4, bc(ident, 1, 4), ALU.add)
                    b = take()
                    for h in range(4):
                        tp = tr(b.ap[:, h * 128:(h + 1) * 128], TT[:, m, h * 128:(h + 1) * 128], t, *b.free)
                    te = acp(TM[:, m, :], b.ap[:, :], tp)
                    give(b, te)
                yield
                tma, tx2 = [None] * 2, [None] * 2
                tT = [A.now()] * 4
                for lv in range(1, 7):
                    for mp in range(0, 4, 2):
                        xs = []
                        for m in (mp, mp + 1):
                            a4 = AT[:, m, :].rearrange("p (h t) -> p h t", h=4)
                            ma = MA[:, m % 2, :]
                            t = stt(ma.rearrange("p (h t) -> p h t", h=4), a4, -1.0, bc(LV[lv], 1, 4),
                                    ALU.mult, ALU.mult, tma[m % 2])
                            b = take()
                            for h in range(4):
                                hs = slice(h * 128, h * 128 + 128)
                                tp = mm(b.ap[:, hs], [(ma[:, hs], TM[:, m, hs])], t, tT[m], *b.free)
                            tma[m % 2] = tp
                            te = acp(XM[:, m % 2, :], b.ap[:, :], tp, tx2[m % 2])
                            give(b, te)
                            xs.append(te)
                        yield
                        for m in (mp, mp + 1):
                            b1, b2 = take(), take()
                            for h in range(4):
                                hs = slice(h * 128, h * 128 + 128)
                                tp = mm(b1.ap[:, hs], [(XM[:, m % 2, hs], TT[:, m, hs])], xs[m % 2], *b1.free)
                                if lv < 6:
                                    tp2 = mm(b2.ap[:, hs], [(TT[:, m, hs], XM[:, m % 2, hs])], *b2.free)
                            if lv < 6:
                                te = tt(TM[:, m, :], TM[:, m, :], b2.ap[:, :], ALU.add, tp2)
                                give(b2, te)
                            else:
                                give(b2, *b2.free)
                            te = tt(TT[:, m, :], TT[:, m, :], b1.ap[:, :], ALU.add, tp if lv == 6 else tp2)
                            give(b1, te)
                            tx2[m % 2] = PE.now()
                            tT[m] = te
                        yield
                NW = KB
                for m in range(4):
                    b = take()
                    for h in range(4):
                        pr, ti = (h % 2) * 64, h // 2
                        tp = mm(b.ap[pr:pr + 64, ti * 128:ti * 128 + 128],
                                [(KG[:, m, 64 * h:64 * h + 64], TT[:, m, h * 128:h * 128 + 128])], tT[3], *b.free)
                    te = ts(NW[:, m, :], b.ap[:, 0:256], -1.0, None, ALU.mult, None, tp)
                    give(b, te)
                yield
                SG = ar(O_HG + 4096, 2, 64)
                VN = ar(O_HG + 4096 + 128, 256)
                V(lambda e: e.memset(SG, 0.0))
                for m in range(4):
                    t = V.now()
                    b, b2, b3 = take(), take(), take()
                    for h in range(4):
                        mm(b.ap[:, 64 * h:64 * h + 64],
                           [(TT[:, m, h * 128:h * 128 + 128], TOK[:, m, 512 + 64 * h:576 + 64 * h])], t, *b.free)
                    for h in HO:
                        pr, ti = (h % 2) * 64, h // 2
                        mm(b.ap[:, 256 + 64 * h:320 + 64 * h],
                           [(NW[pr:pr + 64, m, ti * 128:ti * 128 + 128], SG[pr:pr + 64, ti, :])], rowsw(h))
                        tp = mm(b2.ap[:, 256 + 64 * h:320 + 64 * h],
                                [(TR[pr:pr + 64, m, 6 + ti, :], SG[pr:pr + 64, ti, :])], *b2.free)
                    vcp(VN, b.ap[:, 0:256], tp)
                    te = tt(VN, VN, b.ap[:, 256:512], ALU.add)
                    give(b, te)
                    yield
                    for h in range(4):
                        pr, ti = (h % 2) * 64, h // 2
                        hs = slice(64 * h, 64 * h + 64)
                        mm(b2.ap[:, hs], [(G5[:, m, h * 128:h * 128 + 128], VN[:, hs])], te)
                        tp = mm(b3.ap[pr:pr + 64, ti * 64:ti * 64 + 64], [(TOK[:, m, 256 + 64 * h:320 + 64 * h], VN[:, hs])],
                                *b3.free)
                    vcp(TOK[:, m, 0:256], b2.ap[:, 0:256], tp)
                    te = tt(TOK[:, m, 0:256], TOK[:, m, 0:256], b2.ap[:, 256:512], ALU.add)
                    give(b2, te)
                    for h in range(4):
                        pr, ti = (h % 2) * 64, h // 2
                        te = stt(SG[pr:pr + 64, ti, :], SG[pr:pr + 64, ti, :],
                                 eL[pr:pr + 64, 4 * m + h:4 * m + h + 1],
                                 b3.ap[pr:pr + 64, ti * 64:ti * 64 + 64], ALU.mult, ALU.add)
                    give(b3, te)
                    yield
                OC = ar(O_HG + 4096, 4, 256)
                t = vcp(OC, TOK[:, :, 0:256])
                join()
                yield from finish_c(OC)

            def finish_c(o):
                sq = ar(O_HG, 4, 256)
                sqf = ar(O_HG, 16, 64)
                ss = sm[:, 512:528]
                tt(sq, o, o, ALU.mult)
                red(ss, sqf, ALU.add)
                rstd(ss, 16, 1.0 / 64, 1e-6)
                for m in range(4):
                    q = o[:, m, :].rearrange("p (h d) -> p h d", d=64)
                    tt(q, q, bc(ss[:, 4 * m:4 * m + 4], 2, 64), ALU.mult)
                t = act(sq, CG, ACT.Tanh, V.now(), scale=0.5)
                stt(sq, sq, 1.0, CG, ALU.add, ALU.mult, t)
                t = stt(o, sq, 0.5, o, ALU.mult, ALU.mult)
                yield
                for k in range(2):
                    b = take()
                    for m in range(4):
                        tp = tr(b.ap[:, m * 128:(m + 1) * 128], o[:, m, k * 128:(k + 1) * 128], t, *b.free)
                    g = C1["gain"] + 2 + k
                    te = ts(MIX[:, 6 + k, :], b.ap[:, :], c1[:, g:g + 1], None, ALU.mult, None, tp)
                    give(b, te)
                yield

            V(lambda e: e.memset(CIN[:, :, 0:3], 0.0))
            gemm_t(W, 0, 512, 8, HT, need, ev0)
            gemm_t(W, 512, 256, 8, HT, need, ev1)
            sides.append(attention())
            gemm_c(W, 768, 512, HT, 512, need, ev2)
            gemm_t(W, 1280, 512, 8, HT, need, ev3)
            sides.append(hgrn())
            gemm_c(W, 1792, 512, HT, 512, need, ev_c(0))
            gemm_c(W, 2304, 256, HT, 512, need, ev_c(4))
            gemm_t(W, 2560, 264, 8, HT, need, ev6)
            sides.append(gdn())
            drain()
            join()

            def residual(g, scr, gt):
                tg = s_misc[8].start(P, gt, GTd[0, g, :].partition_broadcast(128), V.now(), A.now(), PE.now(), t_gt)

                def mk(nb):
                    def ev(m, p, t):
                        tmp = scr[:, (m % 2), :]
                        t1 = tt(tmp, p, gt[:, nb * 512:(nb + 1) * 512], ALU.mult, t, tg)
                        xx = X[:, m, nb * 512:(nb + 1) * 512]
                        tt(xx, xx, tmp, ALU.add)
                        return (t1,)
                    return ev
                return mk
            rs = residual(0, ar(0, 2, 512), ar(1024, 1024))
            for nb in range(2):
                gemm_t(T["w_out"][l], nb * 512, 512, 8, MIX, (), rs(nb))
            join()
            norm_stats(X, 1e-6)
            for m in range(4):
                ts(xn[:, m, :], X[:, m, :], sm[:, 600 + m:601 + m], None, ALU.mult)
            need = to_ht(xn, mods[:, 32:40], mods[:, 24:32], V.now())
            join()
            H2 = ar(0, 22, 512)

            def ev_gate(c0):
                def ev(c, p, t):
                    return (act(H2[:, c0 + c, :], p, ACT.Silu, t),)
                return ev

            def ev_up(c0):
                def ev(c, p, t):
                    h = H2[:, c0 + c, :]
                    return (tt(h, h, p, ALU.mult, t, A.now()),)
                return ev
            for nb in range(6):
                nw = min(512, FF - nb * 512)
                gemm_c(T["w_gate"][l], nb * 512, nw, HT, 512, need, ev_gate(4 * nb))
                gemm_c(T["w_up"][l], nb * 512, nw, HT, 512, need, ev_up(4 * nb))
            rs = residual(1, ar(11264, 2, 512), ar(12288, 1024))
            t_h = (V.now(),)
            for nb in range(2):
                gemm_t(T["w_down"][l], nb * 512, 512, 22, H2, t_h, rs(nb))
            join()

        def second(l):
            lam_init = 0.8 - 0.6 * math.exp(-0.3 * l)
            t1 = s_misc[4].start(P, c2[:, :], T["c2"][l], V.now(), A.now())
            t2 = s_misc[5].start(P, r2[:, :], T["r2"][l].partition_broadcast(128), V.now(), A.now())
            join(t1, t2)
            need = to_ht(X, None, None)
            t_xs = s_misc[6].start(P, Xd, X[:, :, :], V.now(), A.now())
            join(t_xs)
            W = T["w_in_2"][l]
            XS = ar(0, 4, 2048)
            Y = ar(8192, 4, 2048)
            BT = X[:, 0:2, :].rearrange("p a (b c) -> p (a b) c", c=512)
            CTt = X[:, 2:4, :].rearrange("p a (b c) -> p (a b) c", c=512)
            BTK = ar(16384, 4, 512)
            STt = ar(18432, 4, 512)
            R4 = 20480
            CV = [ar(R4 + 520 * i, 516) for i in range(2)]
            CO = [ar(R4 + 1040 + 512 * i, 512) for i in range(2)]
            TH = ar(R4 + 2064, 512)
            hw = sm[:, 80:80 + 144]
            ts(hw, c2[:, 0:144], 0.5, None, ALU.mult)
            for i in range(2):
                V(lambda e, i=i: e.memset(CV[i][:, 0:2], 0.0))
                V(lambda e, i=i: e.memset(CV[i][:, 514:516], 0.0))
            st = dict(co=[None, None], cv=[V.now(), V.now()])

            def ev_x(c0):
                def ev(c, p, t):
                    i = c0 + c
                    cv, co = CV[i % 2], CO[i % 2]
                    tf = acp(cv[:, 2:514], p, t, st["cv"][i % 2])
                    ts(co, cv[:, 0:512], hw[:, 5 * i:5 * i + 1], hw[:, 120 + i:121 + i], ALU.mult, ALU.add, tf,
                       st["co"][i % 2])
                    for j in range(1, 5):
                        tv = stt(co, cv[:, j:j + 512], hw[:, 5 * i + j:5 * i + j + 1], co, ALU.mult, ALU.add)
                    st["cv"][i % 2] = tv
                    ta = act(TH, co, ACT.Tanh, tv)
                    if i < 16:
                        dst = co
                    else:
                        dst = (BT if i < 20 else CTt)[:, i % 4, :]
                    tv = stt(dst, TH, 1.0, co, ALU.add, ALU.mult, ta)

                    def later():
                        if i < 20:
                            b = take()
                            for m in range(4):
                                tp = tr(b.ap[:, m * 128:(m + 1) * 128], dst[:, m * 128:(m + 1) * 128], tv, *b.free)
                            o = (XS[:, :, i * 128:(i + 1) * 128] if i < 16 else BTK[:, :, (i - 16) * 128:(i - 15) * 128])
                            te = acp(o, b.ap.rearrange("p (m c) -> p m c", m=4), tp)
                            give(b, te)
                            st["co"][i % 2] = tp
                        return
                        yield
                    sides.append(later())
                    return (tf,)
                return ev

            for nb in range(6):
                gemm_c(W, 2048 + nb * 512, 512, HT, 512, need, ev_x(4 * nb))
            drain()
            DT = sm[:, 80:336].rearrange("p (m h) -> p m h", m=4)

            def ev_dt(m, p, t):
                return (tt(DT[:, m, :], p, r2[:, R2["dtb"]:R2["dtb"] + 64], ALU.add, t),)
            gemm_t(W, 5120, 64, 8, HT, need, ev_dt)

            EF = ar(R4, 8, 128)
            EB = ar(R4 + 1024, 8, 128)
            XF = ar(R4 + 2048, 512)
            XB = ar(R4 + 2560, 512)
            TB = ar(R4 + 3072, 512)
            AA = ar(R4 + 3584, 4, 64)
            AC = ar(R4 + 3840, 4, 64)
            AL = ar(R4 + 4096, 4, 64)
            AB = ar(R4 + 4352, 4, 128)

            def ssd():
                join()
                dt = sm[:, 80:336]
                u = AL.rearrange("p a b -> p (a b)")
                act(u, dt, ACT.Abs)
                act(u, u, ACT.Exp, scale=-1.0)
                act(AC[:, 0, :], r2[:, R2["alog"]:R2["alog"] + 64], ACT.Exp)
                t = act(u, u, ACT.Ln, bias=1.0)
                stt(dt, dt, 0.0, u, ALU.max, ALU.add, t)
                t = stt(AA, DT, -1.0, bc(AC[:, 0, :], 1, 4), ALU.mult, ALU.mult)
                yield
                b = take()
                for m in range(4):
                    mm(b.ap[:, m * 64:m * 64 + 32], [(U, AA[:, m, 0:32])], t, *b.free)
                    mm(b.ap[:, m * 64 + 32:m * 64 + 64], [(Lr, AA[:, m, 32:64])])
                    tp = mm(b.ap[:, 256 + m * 64:256 + m * 64 + 64], [(ones, AA[:, m, :])])
                vcp(AC, b.ap[:, 0:256].rearrange("p (a b) -> p a b", a=4), tp)
                te = vcp(AL, b.ap[:, 256:512].rearrange("p (a b) -> p a b", a=4))
                give(b, te)
                t_ab = [None]
                t_x = [None]
                t_e = [None]
                r3 = lambda z: z.rearrange("p (h d) -> p h d", h=8)
                for m in range(4):
                    for g in range(4):
                        for d, (Ed, ng, tri) in enumerate(((EF, NF, U), (EB, NB, Lr))):
                            for q in range(2):
                                h0 = 32 * d + 8 * g + 4 * q
                                tb = vcp(AB, bc(AA[:, m, h0:h0 + 4], 2, 128), t_ab[0])
                                b = take()
                                for h in range(4):
                                    tp = mm(b.ap[:, h * 128:(h + 1) * 128], [(AB[:, h, :], tri)], tb, *b.free)
                                t_ab[0] = tp
                                for h in range(4):
                                    te = stt(Ed[:, 4 * q + h, :], b.ap[:, h * 128:(h + 1) * 128],
                                             AC[:, m, h0 + h:h0 + h + 1], ng, ALU.subtract, ALU.add, tp, t_e[0])
                                give(b, te)
                                yield
                        ta = act(ar(R4, 2048), ar(R4, 2048), ACT.Exp, te)
                        b = take()
                        tc = mm(b.ap[:, 0:128], [(BT[:, g, m * 128:(m + 1) * 128], CTt[:, g, m * 128:(m + 1) * 128])],
                                *b.free)
                        vcp(TB[:, 0:128], b.ap[:, 0:128], tc)
                        cb = bc(TB[:, 0:128], 1, 8)
                        tt(EF, EF, cb, ALU.mult, ta)
                        te = tt(EB, EB, cb, ALU.mult)
                        give(b, te)
                        xg = XS[:, m, 512 * g:512 * g + 512]
                        for d, xd in enumerate((XF, XB)):
                            tv = tt(r3(xd), r3(xg), bc(DT[:, m, 32 * d + 8 * g:32 * d + 8 * g + 8], 2, 64), ALU.mult, t_x[0])
                        yield
                        b = take()
                        for h in range(8):
                            hs = slice(64 * h, 64 * h + 64)
                            tp = mm(b.ap[:, hs], [(EF[:, h, :], XF[:, hs]), (EB[:, h, :], XB[:, hs])], tv, *b.free)
                        t_x[0] = t_e[0] = tp
                        yg = Y[:, m, 512 * g:512 * g + 512]
                        tt(r3(yg), r3(xg), bc(r2[:, R2["skip"] + 8 * g:R2["skip"] + 8 * g + 8], 2, 64), ALU.mult)
                        te = tt(yg, yg, b.ap[:, :], ALU.add, tp)
                        give(b, te)
                        yield
                join()
                WD = sm[:, 336:592].rearrange("p (m h) -> p m h", m=4)
                t = tt(WD, AL, AC, ALU.subtract)
                t = act(WD, WD, ACT.Exp, t)
                tt(WD, WD, DT, ALU.mult, t)
                t = act(AC, AC, ACT.Exp)
                t = act(AL, AL, ACT.Exp)
                XW = [EF.rearrange("p a b -> p (a b)")[:, 512 * i:512 * i + 512] for i in range(2)]
                t_w = [None, None]
                n = 0
                for d in range(2):
                    order = range(4) if d == 0 else range(3, -1, -1)
                    for ci, m in enumerate(order):
                        for g in range(4):
                            hh = slice(32 * d + 8 * g, 32 * d + 8 * g + 8)
                            xw = XW[n % 2]
                            tv = tt(r3(xw), r3(XS[:, m, 512 * g:512 * g + 512]), bc(WD[:, m, hh], 2, 64), ALU.mult,
                                    t, t_w[n % 2])
                            if ci:
                                b = take()
                                tp = mm(b.ap[:, :], [(CTt[:, g, m * 128:(m + 1) * 128], STt[:, g, :])], t_st[g], *b.free)
                                yg = Y[:, m, 512 * g:512 * g + 512]
                                te = tt(r3(TB), r3(b.ap), bc(AC[:, m, hh], 2, 64), ALU.mult, tp)
                                give(b, te)
                                tt(yg, yg, TB, ALU.add)
                            if ci < 3:
                                b = take()
                                tq = mm(b.ap[:, :], [(BTK[:, m, g * 128:(g + 1) * 128], xw)], tv, *b.free)
                                t_w[n % 2] = tq
                                sg = STt[:, g, :]
                                if ci == 0:
                                    te = vcp(sg, b.ap[:, :], tq)
                                else:
                                    tt(r3(sg), r3(sg), bc(AL[:, m, hh], 2, 64), ALU.mult)
                                    te = tt(sg, sg, b.ap[:, :], ALU.add, tq)
                                give(b, te)
                                if ci == 0 and g == 0:
                                    t_st = [None] * 4
                                t_st[g] = te
                            n += 1
                            yield

            sides.append(ssd())
            STG = ar(25344, 2, 512)
            n_stg = [0]

            def ev_store(dst, n0, kind):
                def ev(m, p, t):
                    i = n_stg[0] % 2
                    n_stg[0] += 1
                    g = STG[:, i, :]
                    free = (s_st[i].sem, s_st[i].n) if s_st[i].n else None
                    if kind == "silu":
                        t = act(g, p, ACT.Tanh, t, free, scale=0.5)
                        t = stt(g, g, 1.0, p, ALU.add, ALU.mult, t)
                        rel = t
                        t = ts(g, g, 0.5, None, ALU.mult)
                    else:
                        rel = t = tt(g, p, GB_[:, n_gb[0] % 2, :], ALU.add, t, free, t_gb[0])
                        t = act(g, g, ACT.Tanh, t, scale=0.5)
                        t = ts(g, g, 1.0, 0.5, ALU.add, ALU.mult, t)
                    s_st[i].start(P, dst[m, :, n0:n0 + 512], g, t)
                    return (rel,)
                return ev
            GB_ = ar(29696, 2, 512)
            n_gb, t_gb = [0], [None]
            for nb in range(4):
                gemm_t(W, nb * 512, 512, 8, HT, need, ev_store(Zd, nb * 512, "silu"))
            for nb in range(6):
                n_gb[0] = nb
                t_gb[0] = s_misc[8 + nb % 2].start(P, GB_[:, nb % 2, :],
                                                   T["gateb"][l][nb * 512:(nb + 1) * 512].partition_broadcast(128), V.now())
                gemm_t(W, 11328 + nb * 512, 512, 8, HT, need, ev_store(Gd, nb * 512, "sig"))
            for nb in range(2):
                gemm_t(W, 8256 + nb * 512, 512, 8, HT, need, ev_store(Dg, nb * 512, "silu"))
            for nb in range(2):
                gemm_t(W, 10304 + nb * 512, 512, 8, HT, need, ev_store(Cg, nb * 512, "silu"))
            drain()
            join()
            stored = [(s.sem, s.n) for s in s_st[0:2]]
            R4 = 24576
            ZT = ar(R4, 2, 2048)
            YT = ar(0, 16, 512)
            SSY = sm[:, 604:608]
            start = fence()
            tq = [None, None]
            for m in range(4):
                zt = ZT[:, m % 2, :]
                tz = s_misc[8 + m % 2].start(P, zt, Zd[m], *stored, tq[m % 2], *(start if m < 2 else ()))
                tv = tt(Y[:, m, :], Y[:, m, :], zt, ALU.mult, tz)
                tq[m % 2] = act(zt, Y[:, m, :], ACT.Square, tv, acc=SSY[:, m:m + 1])
            t = ts(SSY, SSY, 1.0 / 2048, 1e-5, ALU.mult, ALU.add, A.now())
            t = act(SSY, SSY, ACT.Sqrt, t)
            rec(SSY, SSY, t)
            to_ht(Y, c2[:, C2["ssd"]:C2["ssd"] + 16], None, V.now(), dst=YT, nk=16)
            join()

            QT = ar(8192, 8, 512)
            KT = ar(12288, 8, 512)
            DV = ar(16384, 4, 1024)
            OD = ar(20480, 4, 1024)
            MG = X
            RT = ar(R4, 2, 512)
            RM = ar(R4 + 1024, 2, 256)
            n_rt = [0]
            t_rt = [None, None]

            def ev_rope(dst, t0):
                def ev(m, p, t):
                    i = n_rt[0] % 2
                    n_rt[0] += 1
                    q = p.rearrange("p (h u d) -> p h u d", u=2, d=32)
                    o = RT[:, i, :].rearrange("p (h u d) -> p h u d", u=2, d=32)
                    a, b_ = [RM[:, j, :].rearrange("p (h d) -> p h d", d=32) for j in range(2)]
                    cs, sn = bc(tabs[:, m, 16:48], 1, 8), bc(tabs[:, m, 48:80], 1, 8)
                    tt(a, q[:, :, 0, :], cs, ALU.mult, t)
                    tt(b_, q[:, :, 1, :], sn, ALU.mult)
                    tt(o[:, :, 0, :], a, b_, ALU.subtract, t_rt[i])
                    tt(a, q[:, :, 0, :], sn, ALU.mult)
                    tr_ = tt(b_, q[:, :, 1, :], cs, ALU.mult)
                    tv = tt(o[:, :, 1, :], a, b_, ALU.add)

                    def later():
                        b = take()
                        for k in range(4):
                            tp = tr(b.ap[:, k * 128:(k + 1) * 128], RT[:, i, k * 128:(k + 1) * 128], tv, *b.free)
                        te = acp(dst[:, t0:t0 + 4, m * 128:(m + 1) * 128], b.ap.rearrange("p (k c) -> p k c", k=4), tp)
                        give(b, te)
                        t_rt[i] = tp
                        return
                        yield
                    sides.append(later())
                    return (tr_,)
                return ev
            for nb in range(2):
                gemm_t(W, 5184 + nb * 512, 512, 8, HT, need, ev_rope(QT, 4 * nb))
            for nb in range(2):
                gemm_t(W, 6208 + nb * 512, 512, 8, HT, need, ev_rope(KT, 4 * nb))
            drain()

            def ev_dv(n0):
                return lambda m, p, t: (acp(DV[:, m, n0:n0 + 512], p, t),)
            for nb in range(2):
                gemm_t(W, 7232 + nb * 512, 512, 8, HT, need, ev_dv(nb * 512))

            def diff():
                join()
                PB = ar(R4, 2, 2, 512)
                WT = ar(R4 + 2048, 2, 512)
                lm = sm[:, 80:340]
                la = r2[:, R2["lam"]:R2["lam"] + 256]
                tt(lm[:, 0:64], la[:, 0:64], la[:, 64:128], ALU.mult)
                red(lm[:, 256:257], lm[:, 0:64], ALU.add)
                tt(lm[:, 0:64], la[:, 128:192], la[:, 192:256], ALU.mult)
                t = red(lm[:, 257:258], lm[:, 0:64], ALU.add)
                t = act(lm[:, 256:258], lm[:, 256:258], ACT.Exp, t)
                lam = lm[:, 258:259]
                tt(lam, lm[:, 256:257], lm[:, 257:258], ALU.subtract, t)
                ts(lam, lam, lam_init, None, ALU.add)
                mx = sm[:, 344:352].rearrange("p (a b) -> p a b", a=4)
                su = sm[:, 352:360].rearrange("p (a b) -> p a b", a=4)
                st_ = {}
                units = [(h, m) for h in range(8) for m in range(4)]
                t_w = [None, None]
                t_pt = [None, None]

                def front(n):
                    h, m = units[n]
                    i = n % 2
                    for c in range(2):
                        b = take()
                        tp = mm(b.ap[:, :], [(QT[64 * c:64 * c + 64, h, m * 128:(m + 1) * 128],
                                              KT[64 * c:64 * c + 64, h, :])], *b.free)
                        red(mx[:, n % 4, c:c + 1], b.ap[:, :], ALU.max, tp)
                        tv = ts(mx[:, n % 4, c:c + 1], mx[:, n % 4, c:c + 1], -0.125, None, ALU.mult)
                        ta = act(PB[:, i, c, :], b.ap[:, :], ACT.Exp, tv, t_w[i], scale=0.125,
                                 bias=mx[:, n % 4, c:c + 1], acc=su[:, n % 4, c:c + 1])
                        give(b, ta)
                    s = su[:, n % 4, :]
                    rec(s, s, ta)
                    tt(s[:, 1:2], s[:, 1:2], lam, ALU.mult)
                    ts(PB[:, i, 1, :], PB[:, i, 1, :], s[:, 1:2], None, ALU.mult)
                    st_[n] = stt(PB[:, i, 0, :], PB[:, i, 0, :], s[:, 0:1], PB[:, i, 1, :], ALU.mult, ALU.subtract)

                def mid(n):
                    i = n % 2
                    b = take()
                    for k in range(4):
                        tp = tr(b.ap[:, k * 128:(k + 1) * 128], PB[:, i, 0, k * 128:(k + 1) * 128], st_[n], *b.free)
                    t_w[i] = tp
                    te = acp(WT[:, i, :], b.ap[:, :], tp, t_pt[i])
                    give(b, te)
                    st_[n] = te

                def back(n):
                    h, m = units[n]
                    i = n % 2
                    b = take()
                    tp = mm(b.ap[:, 0:128], [(WT[:, i, k * 128:(k + 1) * 128], DV[:, k, h * 128:(h + 1) * 128])
                                             for k in range(4)], st_[n], *b.free)
                    t_pt[i] = tp
                    te = vcp(OD[:, m, h * 128:(h + 1) * 128], b.ap[:, 0:128], tp)
                    give(b, te)
                for n in range(len(units) + 2):
                    if n >= 2:
                        back(n - 2)
                    if 1 <= n <= len(units):
                        mid(n - 1)
                    if n < len(units):
                        front(n)
                    yield
                join()
                DGb = ar(12288, 4, 1024)
                tdg = s_misc[10].start(P, DGb, Dg.rearrange("m p n -> p m n"), V.now(), PE.now(), A.now(), *stored)
                so = sm[:, 80:112]
                sq = ar(8192, 4, 1024)
                tt(sq, OD, OD, ALU.mult)
                red(so, ar(8192, 32, 128), ALU.add)
                rstd(so, 32, 1.0 / 128, 1e-5)
                o3 = ar(20480, 32, 128)
                tt(o3, o3, bc(so, 2, 128), ALU.mult)
                ts(OD, OD, 1.0 - lam_init, None, ALU.mult)
                tt(OD, OD, DGb, ALU.mult, tdg)
                yield
                YD = ar(8192, 8, 512)
                gain = c2[:, C2["diff"]:C2["diff"] + 1]
                t = V.now()
                for k in range(8):
                    b = take()
                    for m in range(4):
                        tp = tr(b.ap[:, m * 128:(m + 1) * 128], OD[:, m, k * 128:(k + 1) * 128], t, *b.free)
                    te = act(YD[:, k, :], b.ap[:, :], ACT.Copy, tp, scale=gain)
                    give(b, te)
                    if k % 2:
                        yield

            sides.append(diff())
            n_g = [0]

            def branch(w, kt, lhs, which, need_, scale=None):
                for nb in range(2):
                    def ev(m, p, t, nb=nb):
                        i = n_g[0] % 2
                        n_g[0] += 1
                        g = GB_[:, i, :]
                        tg = s_misc[8 + i].start(P, g, Gd[m, :, which * 1024 + nb * 512:which * 1024 + nb * 512 + 512],
                                                 V.now(), *stored)
                        mg = MG[:, m, nb * 512:(nb + 1) * 512]
                        if scale is not None:
                            return (stt(mg, p, scale[:, m:m + 1], g, ALU.mult, ALU.mult, t, tg),)
                        r = tt(g, p, g, ALU.mult, t, tg)
                        tt(mg, mg, g, ALU.add)
                        return (r,)
                    gemm_t(w, nb * 512, 512, kt, lhs, need_, ev)

            branch(T["w_br_ssd_2"][l], 16, YT, 0, (), SSY)
            t_yt = PE.now()
            CQ = ar(0, 8, 512)
            MK = ar(4096, 8, 256)
            MV = ar(6144, 2, 1024)
            MT_ = ar(27648, 8, 256)
            tm = s_misc[11].start(P, MT_, T["memT"], *fence())

            def ev_cp(dst, off, wd):
                return lambda c, p, t: (acp(dst[:, off + c, 0:wd], p, t, t_yt),)
            for nb in range(2):
                gemm_c(W, 9280 + nb * 512, 512, HT, 512, need, ev_cp(CQ, 4 * nb, 512))
            for nb in range(2):
                gemm_c(T["w_mem"][l], nb * 512, 512, MT_, 256, (tm,), ev_cp(MK, 4 * nb, 256))
            for nb in range(2):
                gemm_t(T["w_mem"][l], 1024 + nb * 512, 512, 8, MT_, (tm,),
                       lambda m, p, t, nb=nb: (acp(MV[:, m, nb * 512:(nb + 1) * 512], p, t, t_yt),), nm=2)
            drain()
            join()

            def cross():
                CG_ = ar(R4, 4, 1024)
                OC = ar(20480, 4, 1024)
                PX = ar(16384, 4, 256)
                PXT = ar(17408, 2, 512)
                tcg = s_misc[10].start(P, CG_, Cg.rearrange("m p n -> p m n"), V.now(), PE.now(), A.now(), *stored)
                mx, su = sm[:, 80:84], sm[:, 84:88]
                tp = None
                te = None
                for m in range(4):
                    for g in range(2):
                        b = take()
                        for u in range(2):
                            h = 2 * g + u
                            tq = mm(b.ap[:, u * 256:(u + 1) * 256],
                                    [(CQ[:, 2 * h + k, m * 128:(m + 1) * 128], MK[:, 2 * h + k, :]) for k in range(2)],
                                    *b.free)
                        v = b.ap.rearrange("p (u k) -> p u k", u=2)
                        red(mx[:, 2 * g:2 * g + 2], v, ALU.max, tq)
                        tv = tt(PX[:, 2 * g:2 * g + 2, :], v, bc(mx[:, 2 * g:2 * g + 2], 2, 256), ALU.subtract, tp)
                        give(b, tv)
                    ta = act(PX, PX, ACT.Exp, tv, scale=1.0 / 16)
                    red(su, PX, ALU.add, ta)
                    rec(su, su)
                    yield
                    for kt in range(2):
                        b = take()
                        for h in range(4):
                            tp = tr(b.ap[:, h * 128:(h + 1) * 128], PX[:, h, kt * 128:(kt + 1) * 128], ta, *b.free)
                        te = acp(PXT[:, kt, :], b.ap[:, :], tp, te)
                        give(b, te)
                    yield
                    for g in range(2):
                        b = take()
                        for u in range(2):
                            h = 2 * g + u
                            tq = mm(b.ap[:, u * 256:(u + 1) * 256],
                                    [(PXT[:, kt, h * 128:(h + 1) * 128], MV[:, kt, h * 256:(h + 1) * 256]) for kt in range(2)],
                                    te, *b.free)
                        for u in range(2):
                            h = 2 * g + u
                            te2 = stt(OC[:, m, h * 256:(h + 1) * 256], b.ap[:, u * 256:(u + 1) * 256], su[:, h:h + 1],
                                      CG_[:, m, h * 256:(h + 1) * 256], ALU.mult, ALU.mult, tq, tcg)
                        give(b, te2)
                        te = te2
                    yield
                YC = ar(12288, 8, 512)
                t = V.now()
                for k in range(8):
                    b = take()
                    for m in range(4):
                        tp = tr(b.ap[:, m * 128:(m + 1) * 128], OC[:, m, k * 128:(k + 1) * 128], t, *b.free)
                    te = acp(YC[:, k, :], b.ap[:, :], tp)
                    give(b, te)
                    if k % 2:
                        yield
            sides.append(cross())
            branch(T["w_br_diff_2"][l], 8, ar(8192, 8, 512), 1, ())
            drain()
            join()
            branch(T["w_br_cross_2"][l], 8, ar(12288, 8, 512), 2, ())
            join()
            MGT = ar(0, 8, 512)
            to_ht(MG, None, None, dst=MGT)
            join()
            t_xr = s_misc[6].start(P, X[:, :, :], Xd, PE.now(), V.now(), A.now())
            LNG = ar(4096, 1024)
            LNB = ar(5120, 1024)
            t1 = s_misc[4].start(P, LNG, T["lng"][l].partition_broadcast(128), V.now(), A.now(), PE.now())
            t2 = s_misc[5].start(P, LNB, T["lnb"][l].partition_broadcast(128), V.now(), A.now(), PE.now())
            BS = sm[:, 80:128].rearrange("p (m u s) -> p m u s", m=4, u=2)
            MVr = sm[:, 128:136].rearrange("p (m s) -> p m s", m=4)

            def ev_o(nb):
                def ev(m, p, t):
                    xx = X[:, m, nb * 512:(nb + 1) * 512]
                    r = stt(xx, xx, ALPHA, p, ALU.mult, ALU.add, t, t_xr)
                    V(lambda e: e.bn_stats(BS[:, m, nb, :], xx))
                    return (r,)
                return ev
            for nb in range(2):
                gemm_t(T["w_out_2"][l], nb * 512, 512, 8, MGT, (), ev_o(nb))
            for m in range(4):
                V(lambda e, m=m: e.bn_aggr(MVr[:, m, :], BS[:, m, :, :]))
            ts(MVr[:, :, 1], MVr[:, :, 1], 1e-5, None, ALU.add)
            t = act(MVr[:, :, 1], MVr[:, :, 1], ACT.Sqrt, V.now())
            rec(MVr[:, :, 1], MVr[:, :, 1], t)
            for m in range(4):
                ts(X[:, m, :], X[:, m, :], MVr[:, m, 0:1], MVr[:, m, 1:2], ALU.subtract, ALU.mult)
                tt(X[:, m, :], X[:, m, :], LNG, ALU.mult, t1)
                tt(X[:, m, :], X[:, m, :], LNB, ALU.add, t2)
            join()

        PARTS(first, second)
        t = s_misc[7].start(SP, out.rearrange("o (m p) d -> p (o m) d", p=128), X[:, :, :], V.now())
        SP.ops.append(([t] + [(s.sem, s.n) for s in s_st if s.n], None, None, 0))

        block = ctx.enter_context(nc.Block())

        @block.sync
        def _(e):
            SP.emit(e)

        @block.tensor
        def _(e):
            PE.emit(e)

        @block.vector
        def _(e):
            V.emit(e)

        @block.scalar
        def _(e):
            A.emit(e)

        @block.gpsimd
        def _(e):
            P.emit(e)


def PARTS(first, second):
    for l in range(2):
        first(l)
    for l in range(2):
        second(l)


def constants():
    import numpy as np
    r = np.arange(128)
    s, t = r[:, None], r[None, :]
    k = np.zeros((128, NK), np.float32)
    k[:, K_ID:K_ID + 128] = np.eye(128)
    k[:, K_U:K_U + 128] = s <= t
    k[:, K_L:K_L + 128] = s >= t
    k[:, K_NF:K_NF + 128] = np.where(s <= t, 0.0, -1e30)
    k[:, K_NB:K_NB + 128] = np.where(s >= t, 0.0, -1e30)
    k[:, K_ONE:K_ONE + 128] = 1.0
    k[:, K_AM:K_AM + 128] = np.where(t > s, 0.0, -1e30)
    k[:, K_AM + 128:K_AM + 256] = np.where(t <= s, 0.0, -1e30)
    for i in range(7):
        b = 1 << i
        k[:, K_LV + 128 * i:K_LV + 128 * i + 128] = (t // b == s // b + 1) & (t // (2 * b) == s // (2 * b))
    k[:, K_F8:K_F8 + 8] = 500000.0 ** (-np.arange(8, dtype=np.float64) * 2.0 / 16)
    k[:, K_F32:K_F32 + 32] = 10000.0 ** (-np.arange(0, 64, 2, dtype=np.float64) / 64)
    return k


def layout(i):
    import numpy as np
    cols = lambda v: np.ascontiguousarray(np.asarray(v).reshape(-1, 128).T)
    a = {k: np.asarray(v) for k, v in i.items()}
    o = {"cst": constants(), "x": a["x"], "c": cols(a["c"]),
         "pos": np.concatenate([cols(a["positions"]), cols(a["positions_2"])], 1)}
    c1, r1, c2, r2, gtb = [], [], [], [], []
    for l in range(2):
        conv = a["gdn_conv_w"][l].reshape(4, 6, 128).transpose(2, 1, 0).reshape(128, 24)
        hg, gd = a["hgrn_out_norm"][l], a["gdn_out_norm"][l]
        gain = np.stack([np.tile(hg, 2)] * 2 + [np.tile(gd, 2)] * 2, 1)
        c1.append(np.concatenate([cols(a["norm_mix"][l]), cols(a["norm_ffn"][l]), cols(a["ada_b"][l]),
                                  cols(a["hgrn_lb_logits"][0]), cols(a["hgrn_lb_logits"][1]), conv, gain], 1))
        r1.append(np.concatenate([a["attn_q_norm"][l], a["attn_k_norm"][l], a["attn_sinks"][l],
                                  a["gdn_a_log"][l], a["gdn_dt_bias"][l]]))
        cv2 = a["conv_w_2"][l].reshape(5, 24, 128).transpose(2, 1, 0).reshape(128, 120)
        c2.append(np.concatenate([cv2, cols(a["conv_b_2"][l]), cols(a["ssd_norm_w_2"][l]),
                                  cols(a["diff_norm_w_2"][l])], 1))
        r2.append(np.concatenate([a["dt_bias_2"][l].ravel(), a["a_log_2"][l].ravel(), a["d_skip_2"][l],
                                  a["diff_lam_2"][l].ravel()]))
        gtb.append(np.concatenate([a["ada_b"][l][2048:3072], a["ada_b"][l][5120:6144]]))
    o.update(c1=np.stack(c1), r1=np.stack(r1), c2=np.stack(c2), r2=np.stack(r2), gtb=np.stack(gtb))
    for n in ("ada_w", "w_in", "w_gate", "w_up", "w_down", "w_in_2", "w_br_ssd_2", "w_br_diff_2", "w_br_cross_2",
              "w_out_2"):
        o[n] = a[n]
    o["w_mem"] = a["w_mem_kv_2"]
    wo = a["w_out"]
    top = wo[:, 0:512].reshape(2, 2, 4, 64, 1024).transpose(0, 2, 1, 3, 4).reshape(2, 512, 1024)
    o["w_out"] = np.concatenate([top, wo[:, 512:]], 1)
    o["memT"] = np.ascontiguousarray(a["mem_2"][0].T.reshape(8, 128, 256).transpose(1, 0, 2))
    o["gateb"] = a["gate_b_2"].reshape(2, 3072)
    o["lng"], o["lnb"] = a["ln_g_2"], a["ln_b_2"]
    return o


def kernel(**inputs):
    import numpy as np
    import concourse.bacc as bacc
    from concourse.bass_utils import run_bass_kernel_spmd as run

    nc = bacc.Bacc("TRN2", target_bir_lowering=False, num_devices=1)
    arrays, T = {}, {}
    for name, v in layout(inputs).items():
        v = np.ascontiguousarray(v)
        arrays["in_" + name] = v
        T[name] = nc.dram_tensor("in_" + name, v.shape, mybir.dt.from_np(v.dtype), kind="ExternalInput").ap()
    out = nc.dram_tensor("out_0", (1, S, D), F32, kind="ExternalOutput").ap()
    program(nc, T, out)
    r = run(nc, [arrays], core_ids=[0])
    return r.results[0]["out_0"]
```

```python
import math
from contextlib import ExitStack

import concourse.bass as bass
from concourse import mybir

F32 = mybir.dt.float32
F32R = mybir.dt.float32r
I32 = mybir.dt.int32
ALU = mybir.AluOpType
ACT = mybir.ActivationFunctionType
AX = mybir.AxisListType.X

D = 1024
S = 512
FF = 2816
N_IN1 = 2824
N_IN2 = 14400
ALPHA = 4.0 ** 0.25
TWO_PI = 2.0 * math.pi
RING = 3
NSP = 4
SLACK = 1.5
STEPS = 3
KS = 2
ARENA = 25732

C1 = dict(nmix=0, nffn=8, adab=16, lb0=64, lb1=66, conv=68, gain=92)
NC1 = 96
C2 = dict(conv=0, cb=120, ssd=144, diff=160)
NC2 = 161
R1 = dict(qn=0, kn=64, sink=128, alog=136, dtb=140)
NR1 = 144
R2 = dict(dtb=0, alog=64, skip=128, lam=160)
NR2 = 416
K_ID, K_U, K_L, K_ONE, K_AM, K_NB, K_LV = 0, 128, 256, 384, 512, 640, 768
K_F8, K_F32 = K_LV + 7 * 128, K_LV + 7 * 128 + 8
K_NF = K_F32 + 32
NK = K_NF + 128


DUE = {}


def due(token):
    return DUE.get((token[0].name, token[1]), 0.0)


def width(ap):
    n = 1
    for s in ap.shape[1:]:
        n *= s
    return n


class Queue:

    def __init__(self, sem, chain):
        self.sem, self.chain, self.n, self.ops, self.t = sem, chain, 0, [], 0.0

    def __call__(self, fn, *waits, inc=True, par=False, us=0.3):
        w = [t for t in waits if t is not None]
        if self.chain and self.n and not par:
            w.append((self.sem, self.n))
        self.ops.append((w, fn, self.sem if inc else None, 1))
        self.t = max([self.t] + [due(x) + 0.1 for x in w]) + us
        if inc:
            self.n += 1
            DUE[self.sem.name, self.n] = self.t
        return (self.sem, self.n)

    def now(self):
        return (self.sem, self.n) if self.n else None

    def emit(self, eng):
        seen = {}
        for waits, fn, sem, by in self.ops:
            for s, v in waits:
                if seen.get(s.name, 0) < v:
                    eng.wait_ge(s, v)
                    seen[s.name] = v
            ins = fn(eng) if fn else None
            if sem is not None:
                ins.then_inc(sem, by)


class Load:

    def __init__(self, sem):
        self.sem, self.n = sem, 0

    def start(self, q, out, in_, *waits):
        w = [t for t in waits if t is not None]
        if self.n:
            w.append((self.sem, self.n))
        q.ops.append((w, lambda e: e.dma_start(out, in_), self.sem, 16))
        self.n += 16
        DUE[self.sem.name, self.n] = max([0.0] + [due(x) for x in w]) + 4.0
        return (self.sem, self.n)


class Bank:
    def __init__(self, ap):
        self.ap, self.free = ap, ()


def bc(ap, axis, n):
    v = ap.unsqueeze(axis)
    shape = list(v.shape)
    shape[axis] = n
    return v.to_broadcast(shape)


def program(nc, T, out):
    DUE.clear()
    ctx = ExitStack()
    with ctx:
        def sb(name, shape, dt=F32):
            return ctx.enter_context(nc.sbuf_tensor(name, shape, dt))

        def sem(name):
            return ctx.enter_context(nc.semaphore(name))

        cst = sb("cst", [128, K_NF])
        X = sb("X", [128, 4, D])
        with nc.sbuf_tensor("HTh", [128, 8, S], F32R) as hh, nc.sbuf_tensor("HTl", [128, 8, S], F32R) as hl:
            HT = (hh, hl)
        HF = sb("HF", [128, 2, 4096])
        SPL = [(sb(f"sph{i}", [128, KS, 512], F32R), sb(f"spl{i}", [128, KS, 512], F32R)) for i in range(NSP)]
        RG = [sb(f"ring{i}", [128, KS, 512]) for i in range(RING)]
        AR = sb("arena", [128, ARENA])
        c2 = sb("c2", [128, NC2])
        r2 = sb("r2", [128, NR2])
        c1s = sb("c1", [128, 2, NC1])
        modt = sb("modt", [128, 2, 48])
        r1 = r2[:, 0:NR1]
        NFr = [sb(f"nfr{i}", [128, 128], F32R) for i in range(3)]
        sm = sb("sm", [128, 608])
        tabs = sb("tabs", [128, 4, 80])
        pos = sb("pos", [128, 8], I32)
        Zd = nc.dram_tensor("zd", (4, 128, 2048), F32, kind="Internal").ap()
        Gd = nc.dram_tensor("gd", (4, 128, 3072), F32, kind="Internal").ap()
        Dg = nc.dram_tensor("dgd", (4, 128, 1024), F32, kind="Internal").ap()
        Cg = nc.dram_tensor("cgd", (4, 128, 1024), F32, kind="Internal").ap()
        GTd = nc.dram_tensor("gtd", (2, 2048), F32, kind="Internal").ap()
        KVd = nc.dram_tensor("kvd", (2, 128, 4096), F32, kind="Internal").ap()
        Xd = nc.dram_tensor("xd", (128, 4, 1024), F32, kind="Internal").ap()
        banks = [Bank(ctx.enter_context(nc.psum_tensor(f"ps{i}", [128, 512], F32))) for i in range(8)]

        PE = Queue(sem("s_pe"), False)
        V = Queue(sem("s_dve"), True)
        A = Queue(sem("s_act"), True)
        P = Queue(sem("s_pool"), True)
        SP = Queue(sem("s_sp"), False)

        s_misc = [Load(sem(f"s_misc{i}")) for i in range(12)]
        s_ring = [Load(sem(f"s_ring{i}")) for i in range(RING)]
        s_g = [Load(sem(f"s_g{i}")) for i in range(6)]
        s_st = [Load(sem(f"s_st{i}")) for i in range(4)]

        ident = cst[:, K_ID:K_ID + 128]
        U = cst[:, K_U:K_U + 128]
        Lr = cst[:, K_L:K_L + 128]
        NF = AR[:, 0:128]
        NB = cst[:, K_NB:K_NB + 128]
        ones = cst[:, K_ONE:K_ONE + 128]
        AM = cst[:, K_AM:K_AM + 256]
        LV = [cst[:, K_LV + 128 * i:K_LV + 128 * (i + 1)] for i in range(7)]

        def ar(off, *shape):
            n = 1
            for s in shape:
                n *= s
            assert off + n <= ARENA, (off, n)
            v = AR[:, off:off + n]
            if len(shape) == 2:
                v = v.rearrange("p (a b) -> p a b", a=shape[0])
            elif len(shape) == 3:
                v = v.rearrange("p (a b c) -> p a b c", a=shape[0], b=shape[1])
            return v

        def tt(o, a, b, op, *w, par=False):
            return V(lambda e: e.tensor_tensor(o, a, b, op), *w, par=par, us=0.08 + width(o) / 960)

        def ts(o, a, s1, s2, op0, op1=None, *w, par=False):
            us = 0.08 + width(o) / 1200
            if op1 is None:
                return V(lambda e: e.tensor_scalar(o, a, s1, None, op0), *w, par=par, us=us)
            return V(lambda e: e.tensor_scalar(o, a, s1, s2, op0, op1), *w, par=par, us=us)

        def stt(o, a, s1, b, op0, op1, *w, par=False):
            return V(lambda e: e.scalar_tensor_tensor(out=o, in0=a, scalar=s1, in1=b, op0=op0, op1=op1), *w,
                     par=par, us=0.08 + width(o) / 960)

        def red(o, a, op, *w, par=False):
            return V(lambda e: e.tensor_reduce(o, a, AX, op), *w, par=par, us=0.08 + width(a) / 960)

        def rec(o, a, *w, par=False):
            return V(lambda e: e.reciprocal(o, a), *w, par=par, us=0.08 + width(o) / 200)

        def vcp(o, a, *w, par=False):
            return V(lambda e: e.tensor_copy(o, a), *w, par=par, us=0.08 + width(o) / 1200)

        def act(o, a, f, *w, scale=1.0, bias=None, acc=None, par=False):
            kw = dict(scale=scale)
            if bias is not None:
                kw["bias"] = bias
            if acc is not None:
                kw["accum_out"] = acc
            return A(lambda e: e.activation(o, a, f, **kw), *w, par=par, us=0.2 + width(o) / 1400)

        def acp(o, a, *w, par=False):
            return act(o, a, ACT.Copy, *w, par=par)

        def take():
            assert banks, "every bank is held"
            return banks.pop(0)

        def give(b, *tokens):
            b.free = tokens
            banks.append(b)

        def mm(o, pairs, *w):
            for i, (l, r) in enumerate(pairs):
                st, sp = i == 0, i == len(pairs) - 1
                t = PE(lambda e, l=l, r=r, st=st, sp=sp: e.matmul(o, l, r, start=st, stop=sp),
                       *(w if st else ()), inc=sp, us=max(width(r) / 596, 0.21))
            return t

        def tr(o, i, *w):
            return PE(lambda e: e.transpose(o, i, ident), *w, us=0.21)

        def rstd(buf, n, scale, eps):
            a = ts(buf, buf, scale, eps, ALU.mult, ALU.add)
            b = act(buf, buf, ACT.Sqrt, a)
            return rec(buf, buf, b)

        HO = (0, 2, 1, 3)

        def rowsw(h):
            return PE.now() if h == 1 else None

        sides = []

        done = set()

        def side(name, gen, after=()):
            sides.append([name, gen, after, max(V.t, A.t)])

        def pump(force=False):
            can = [x for x in sides if all(a in done for a in x[2])]
            if not can:
                return False
            x = min(can, key=lambda x: x[3])
            if x[3] > PE.t + SLACK and not force:
                return False
            sides.remove(x)
            try:
                next(x[1])
                x[3] = max(V.t, A.t)
                sides.append(x)
            except StopIteration:
                done.add(x[0])
            return True

        def drain():
            while sides:
                pump(True)

        slot_free = [()] * RING
        n_slot = [0]

        def wload(src, kk, nw):
            i = n_slot[0] % RING
            n_slot[0] += 1
            v = RG[i][:, 0:kk, 0:nw]
            t = s_ring[i].start(SP, v, src, *slot_free[i])
            return i, v, t

        sp_free = [()] * NSP
        n_sp = [0]

        def split(src, *toks):
            i = n_sp[0] % NSP
            n_sp[0] += 1
            kk, n = src.shape[1], src.shape[2]
            h, lo = SPL[i][0][:, 0:kk, 0:n], SPL[i][1][:, 0:kk, 0:n]
            ta = acp(h, src, *toks, *sp_free[i], par=True)
            tv = tt(lo, src, h.bitcast(F32), ALU.subtract, ta, par=True)
            return i, h, lo, tv

        jobs = []

        def then(fn, block=False):
            jobs.append((None, fn, -1 if block else 0))

        ahead = {}

        def warm(k=NSP - 1):
            for n in range(k):
                ahead[n] = jobs[n][0]()

        def flush():
            pre = {n: (v, max(jobs[n][2], 0)) for n, v in ahead.items()}
            nxt = len(pre)
            ahead.clear()
            for n in range(len(jobs)):
                used = sum(v[1] for v in pre.values())
                while nxt < len(jobs):
                    prep, _, cost = jobs[nxt]
                    if nxt > n and cost > 0 and used + cost > (NSP - 1 if cost == 1 else NSP):
                        break
                    if nxt > n + 8 or (nxt > n and jobs[n:nxt] and any(j[2] < 0 for j in jobs[n:nxt])):
                        break
                    pre[nxt] = (prep() if prep else None, max(cost, 0))
                    used += max(cost, 0)
                    nxt += 1
                st, _ = pre.pop(n)
                jobs[n][1](st)
            jobs.clear()

        def operand(src, k0, kk, n, need):
            if isinstance(src, tuple):
                return None, src[0][:, k0:k0 + kk, 0:n], src[1][:, k0:k0 + kk, 0:n], None
            return split(src[:, k0:k0 + kk, 0:n], *(need(k0) if callable(need) else need))

        def gemm(w, n0, nw, kt, act_, need, evict, nt, by_token, ns=512):
            held = [None] * 4
            for k0 in range(0, kt, KS):
                def prep(k0=k0):
                    i, v, t = wload(w[k0 * 128:(k0 + KS) * 128, n0:n0 + nw].rearrange("(k p) n -> p k n", p=128), KS, nw)
                    sw = split(v, t)
                    slot_free[i] = (sw[3],)
                    return sw, operand(act_, k0, KS, ns, need)

                def run(st, k0=k0):
                    (wi, wh, wl, wt), (xi, xh, xl, xt) = st
                    toks = [wt, xt] + (list(need) if k0 == 0 and not callable(need) else [])
                    while due(wt) > PE.t + SLACK and pump():
                        pass
                    for m in range(nt):
                        if k0 == 0:
                            held[m] = take()
                        b = held[m]
                        o = b.ap[:, 0:nw] if by_token else b.ap[:, 0:ns]
                        ms = slice(m * 128, (m + 1) * 128)
                        n = 0
                        for k in range(KS):
                            for p, q in ((0, 0), (0, 1), (1, 0)):
                                ww, xx = (wh, wl)[p], (xh, xl)[q]
                                l, r = (xx[:, k, ms], ww[:, k, :]) if by_token else (ww[:, k, ms], xx[:, k, :])
                                first, last = k0 == 0 and n == 0, k0 + KS == kt and n == 3 * KS - 1
                                wait = (*toks, *(b.free if k0 == 0 else ())) if n == 0 else ()
                                tok = PE(lambda e, o=o, l=l, r=r, first=first, last=last: e.matmul(
                                    o, l, r, start=first, stop=last), *wait, inc=(n == 3 * KS - 1), us=width(r) / 2400)
                                n += 1
                        if k0 + KS == kt:
                            give(b, *evict(m, o, tok))
                        for _ in range(STEPS):
                            if not pump():
                                break
                    sp_free[wi] = (tok,)
                    if xi is not None:
                        sp_free[xi] = (tok,)
                jobs.append((prep, run, 1 if isinstance(act_, tuple) else 2))

        def gemm_t(w, n0, nw, kt, lhs, need, evict, nm=4):
            gemm(w, n0, nw, kt, lhs, need, evict, nm, True, nm * 128)

        def gemm_c(w, n0, nw, rhs, ns, need, evict):
            gemm(w, n0, nw, 8, rhs, need, evict, nw // 128, False, ns)

        def fence():
            return [q.now() for q in (PE, V, A)]

        def join(*extra):
            f = [x for x in fence() if x] + [x for x in extra if x]
            for q in (PE, V, A):
                q.ops.append((f, None, None, 0))
                q.t = max([q.t] + [due(x) for x in f])

        t_cst = s_misc[0].start(SP, cst[:, :], T["cst"][:, 0:K_NF])
        t_nf = s_misc[9].start(P, NF, T["cst"][:, K_NF:NK])
        t_pos = s_misc[1].start(SP, pos[:, :], T["pos"])
        t_x = s_misc[2].start(SP, X[:, :, :], T["x"].rearrange("o (m p) d -> p (o m) d", p=128))
        cc = sm[:, 0:8]
        t_c = s_misc[3].start(SP, cc, T["c"])
        t_c1 = s_misc[7].start(SP, c1s[:, :, :], T["c1"].rearrange("l p n -> p l n"))
        join(t_cst, t_nf, t_pos, t_x, t_c, t_c1)
        for i, src in enumerate((ident, NF, NB)):
            acp(NFr[i][:, :], src)
        cond = sm[:, 8:16]
        t = act(cond, cc, ACT.Tanh, scale=0.5)
        t = stt(cond, cond, 1.0, cc, ALU.add, ALU.mult, t)
        ts(cond, cond, 0.5, None, ALU.mult)

        MAGIC = 12582912.0
        C_A, C_B = 6.28125, 0.0019340515136718750
        C_C = TWO_PI - C_A - C_B
        pf = sm[:, 16:24]
        vcp(pf, pos[:, :])
        for which, (n, o, kf) in enumerate(((8, 0, K_F8), (32, 16, K_F32))):
            for m in range(4):
                ang = sm[:, 32:32 + n]
                rn = sm[:, 64:64 + n]
                ts(ang, cst[:, kf:kf + n], pf[:, 4 * which + m:4 * which + m + 1], None, ALU.mult)
                for cos in (1, 0):
                    dst = tabs[:, m, o + (0 if cos else n):o + (0 if cos else n) + n]
                    ts(rn, ang, 1.0 / TWO_PI, 0.25 * cos, ALU.mult, ALU.add)
                    ts(rn, rn, MAGIC, None, ALU.add)
                    ts(rn, rn, -MAGIC, None, ALU.add)
                    stt(dst, rn, -C_A, ang, ALU.mult, ALU.add)
                    stt(dst, rn, -C_B, dst, ALU.mult, ALU.add)
                    stt(dst, rn, -C_C, dst, ALU.mult, ALU.add)
                    ts(dst, dst, math.pi / 2 * cos, None, ALU.add)
                    ts(dst, dst, 3.1415925, -3.1415925, ALU.min, ALU.max)
        t = V.now()
        for m in range(4):
            act(tabs[:, m, :], tabs[:, m, :], ACT.Sin, t)

        def norm_stats(src, eps):
            j = ar(ARENA - 1024, 1024)
            for m in range(4):
                act(j, src[:, m, :], ACT.Square, V.now(), acc=sm[:, 600 + m:601 + m])
            a = ts(sm[:, 600:604], sm[:, 600:604], 1.0 / D, eps, ALU.mult, ALU.add, A.now())
            b = act(sm[:, 600:604], sm[:, 600:604], ACT.Sqrt, a)
            rec(sm[:, 600:604], sm[:, 600:604], b)

        def to_ht(src, scale, bias, scr, *w):
            pend = [None, None]
            for k in range(8):
                b = take()
                for m in range(4):
                    t = tr(b.ap[:, m * 128:(m + 1) * 128], src[:, m, k * 128:(k + 1) * 128],
                           *(b.free if m == 0 else ()), *w)
                f = scr[:, k % 2, :]
                if scale is None:
                    t = (acp if k % 2 else vcp)(f, b.ap[:, :], t, pend[k % 2], par=k > 1)
                elif k % 2:
                    t = act(f, b.ap[:, :], ACT.Identity, t, pend[1], scale=scale[:, k:k + 1], bias=bias[:, k:k + 1],
                            par=k > 1)
                else:
                    t = ts(f, b.ap[:, :], scale[:, k:k + 1], bias[:, k:k + 1], ALU.mult, ALU.add, t, pend[0],
                           par=k > 1)
                give(b, t)
                t = acp(HT[0][:, k, :], f, t, par=True)
                pend[k % 2] = tt(HT[1][:, k, :], f, HT[0][:, k, :].bitcast(F32), ALU.subtract, t, par=True)
            return (V.now(), A.now())

        def turn(src, dst, nk, scale=None, tok=None):
            for k in nk:
                b = take()
                for m in range(4):
                    t = tr(b.ap[:, m * 128:(m + 1) * 128], src[:, m, k * 128:(k + 1) * 128], tok, *b.free)
                if scale is None:
                    t = acp(dst[:, k, :], b.ap[:, :], t, par=True) if k % 2 else vcp(dst[:, k, :], b.ap[:, :], t, par=True)
                else:
                    sc = scale[:, k:k + 1]
                    t = ts(dst[:, k, :], b.ap[:, :], sc, None, ALU.mult, None, t, par=True) if k % 2 else \
                        act(dst[:, k, :], b.ap[:, :], ACT.Copy, t, scale=sc, par=True)
                give(b, t)

        O_ATT, O_HG, O_C = 0, 7680, 7680 + 9344
        O_MIX = O_C + 516 + 3072 + 1024
        t_kv = {}
        t_gt = {}
        ada_pend = {}

        def ada(l, blocks, scr):
            c1 = c1s[:, l, :]
            for nb in blocks:
                acc, row = scr[nb % 3], scr[3]
                part = nb // 2
                for k0 in range(0, 8, KS):
                    def prep(k0=k0, acc=acc, nb=nb):
                        i, v, t = wload(T["ada_w"][l][k0 * 128:(k0 + KS) * 128, nb * 512:(nb + 1) * 512].rearrange(
                            "(k p) n -> p k n", p=128), KS, 512)
                        for k in range(k0, k0 + KS):
                            if k == 0:
                                tv = ts(acc, v[:, 0, :], cond[:, 0:1], None, ALU.mult, None, t, ada_pend.get(nb % 3))
                            else:
                                tv = stt(acc, v[:, k - k0, :], cond[:, k:k + 1], acc, ALU.mult, ALU.add, t)
                        slot_free[i] = (tv,)
                        return tv

                    def run(tv, nb=nb, part=part, acc=acc, row=row):
                        b = take()
                        if part in (2, 5):
                            n0 = (part // 3) * 1024 + (nb % 2) * 512
                            tr_ = s_misc[8].start(P, row, T["gtb"][l][n0:n0 + 512].partition_broadcast(128),
                                                  V.now(), (s_st[2].sem, s_st[2].n) if s_st[2].n else None)
                            tp = mm(b.ap[:, :], [(ones, acc)], tv, *b.free)
                            te = tt(row, b.ap[:, :], row, ALU.add, tp, tr_)
                            t_gt[l] = s_st[2].start(P, GTd[l:l + 1, n0:n0 + 512], row[0:1, :], te)
                        else:
                            for j in range(4):
                                tp = mm(b.ap[:, j:j + 1], [(acc[:, j * 128:(j + 1) * 128], ones[:, 0:1])], tv, *b.free)
                            md = modt[:, l, nb * 4:nb * 4 + 4]
                            te = tt(md, b.ap[:, 0:4], c1[:, C1["adab"] + nb * 4:C1["adab"] + nb * 4 + 4], ALU.add, tp)
                            if part in (1, 4):
                                g0 = C1["nmix" if part == 1 else "nffn"] + (nb % 2) * 4
                                stt(md, md, 1.0, c1[:, g0:g0 + 4], ALU.add, ALU.mult)
                        ada_pend[nb % 3] = tp
                        give(b, te)
                    jobs.append((prep, run if k0 + KS == 8 else (lambda st: None), 0))

        def weave(first, second):
            out = []
            while first or second:
                if first:
                    out.append(first.pop(0))
                if second:
                    out.append(second.pop(0))
            return out

        def memory(l):
            MT_ = HF[:, 0, 0:2048].rearrange("p (b c) -> p b c", c=256)
            KVs = HF[:, 1, 0:2048]
            MKf, MVf = KVs.rearrange("p (a b) -> p a b", a=8), KVs.rearrange("p (a b) -> p a b", a=2)
            tm, free, last = [], [], []

            def start(st):
                free.append(PE.now())
                tm.append(s_misc[11].start(P, MT_, T["memT"], *free))

            def ev_k(nb):
                def ev(c, p, t):
                    last.append(acp(MKf[:, 4 * nb + c, :], p, t, *free))
                    return (last[-1],)
                return ev

            def mid(st):
                free.append(s_st[3].start(P, KVd[l, :, 0:2048], KVs, last[-1]))

            def ev_v(nb):
                def ev(m, p, t):
                    last.append(acp(MVf[:, m, nb * 512:(nb + 1) * 512], p, t, *free))
                    return (last[-1],)
                return ev

            def end(st):
                t_kv[l] = s_st[3].start(P, KVd[l, :, 2048:4096], KVs, last[-1])
            then(start, True)
            for nb in range(2):
                gemm_c(T["w_mem"][l], nb * 512, 512, MT_, 256, tm, ev_k(nb))
            then(mid)
            for nb in range(2):
                gemm_t(T["w_mem"][l], 1024 + nb * 512, 512, 8, MT_, tm, ev_v(nb), nm=2)
            then(end)

        def first(l):
            c1 = c1s[:, l, :]
            mods = modt[:, l, :]

            def scale_row(m):
                s = sm[:, 600 + m:601 + m]
                if m % 2:
                    act(xn[:, m, :], X[:, m, :], ACT.Copy, V.now(), scale=s)
                else:
                    ts(xn[:, m, :], X[:, m, :], s, None, ALU.mult)
            t2 = s_misc[5].start(P, r1, T["r1"][l].partition_broadcast(128), *fence())
            t_xs = s_misc[6].start(P, Xd, X[:, :, :], *fence())
            if l == 0:
                ada(0, range(4), [ar(2048 + 512 * i, 512) for i in range(4)])
                flush()
            join(t2)
            need = []
            W = T["w_in"][l]
            MIX = ar(O_MIX, 8, 512)

            if l == 0:
                ada(0, range(4, 12), [ar(O_HG + 7168 + 512 * i, 512) for i in range(4)])
                extra, jobs[:] = list(jobs), []
            else:
                extra = []
            QK = ar(O_ATT, 4, 640)
            QKT = ar(O_ATT + 2560, 5, 512)
            AV = ar(O_ATT + 5120, 4, 128)
            PT = ar(O_ATT + 5632, 4, 512)
            BQ, Zb, BV, BG, KT, E_, XL = [ar(O_HG + 1024 * i, 1024) for i in range(7)]
            ACC = ar(O_HG + 7168, 4, 512)
            ST = ar(O_HG + 9216, 2, 64)
            BQ3, Z3, KT3 = [z.rearrange("p (a b) -> p a b", a=2) for z in (BQ, Zb, KT)]
            BV3, BG3 = [z.rearrange("p (a b) -> p a b", a=4) for z in (BV, BG)]
            CIN = ar(O_C, 516)
            CT = ar(O_C + 516, 6, 512)
            CG = ar(O_C + 516 + 3072, 4, 256)
            CBA = sm[:, 80:112].rearrange("p (a b) -> p a b", a=4)

            def ev0(m, p, t):
                o = QK[:, m, 0:512].rearrange("p (i j d) -> p j i d", i=4, j=2)
                return (vcp(o, p.rearrange("p (j i d) -> p j i d", j=2, i=4), t, par=True),)

            def ev1(m, p, t):
                acp(QK[:, m, 512:640], p[:, 0:128], t, par=True)
                return (acp(AV[:, m, :], p[:, 128:256], t, par=True),)

            def ev2(c, p, t):
                return (acp((BQ3, Z3)[c // 2][:, c % 2, :], p, t, par=True),)

            def ev3(m, p, t):
                acp(BV3[:, m, :], p[:, 0:256], t, par=True)
                return (acp(BG3[:, m, :], p[:, 256:512], t, par=True),)

            def ev_c(c0):
                def ev(c, p, t):
                    i = c0 + c
                    tf = acp(CIN[:, 3:515], p, t, V.now())
                    ts(CT[:, i, :], CIN[:, 0:512], hw[:, 4 * i:4 * i + 1], None, ALU.mult, None, tf)
                    for j in range(1, 4):
                        tv = stt(CT[:, i, :], CIN[:, j:j + 512], hw[:, 4 * i + j:4 * i + j + 1], CT[:, i, :],
                                 ALU.mult, ALU.add)
                    ta = act(CIN[:, 3:515], CT[:, i, :], ACT.Tanh, tv)
                    stt(CT[:, i, :], CIN[:, 3:515], 1.0, CT[:, i, :], ALU.add, ALU.mult, ta)
                    return (tf,)
                return ev

            def ev6(m, p, t):
                acp(CG[:, m, :], p[:, 0:256], t, par=True)
                return (acp(CBA[:, m, :], p[:, 256:264], t, par=True),)

            def attention():
                join()
                sq = PT.rearrange("p a b -> p (a b)")[:, 0:640]
                ss = sm[:, 120:160]
                for m in range(4):
                    tt(sq, QK[:, m, :], QK[:, m, :], ALU.mult)
                    red(ss[:, m * 10:m * 10 + 10], sq.rearrange("p (h d) -> p h d", d=64), ALU.add)
                rstd(ss, 40, 1.0 / 64, 1e-6)
                rt = [sm[:, 160 + 80 * i:240 + 80 * i].rearrange("p (h d) -> p h d", d=8) for i in range(4)]
                for m in range(4):
                    q = QK[:, m, :].rearrange("p (h d) -> p h d", d=64)
                    tt(q, q, bc(ss[:, m * 10:m * 10 + 10], 2, 64), ALU.mult)
                    tt(q[:, 0:8, :], q[:, 0:8, :], bc(r1[:, R1["qn"]:R1["qn"] + 64], 1, 8), ALU.mult)
                    tt(q[:, 8:10, :], q[:, 8:10, :], bc(r1[:, R1["kn"]:R1["kn"] + 64], 1, 2), ALU.mult)
                    cs, sn = bc(tabs[:, m, 0:8], 1, 10), bc(tabs[:, m, 8:16], 1, 10)
                    x1, x2 = q[:, :, 0:8], q[:, :, 8:16]
                    tt(rt[0], x1, cs, ALU.mult)
                    tt(rt[1], x2, sn, ALU.mult, par=True)
                    tt(rt[2], x2, cs, ALU.mult, par=True)
                    tt(rt[3], x1, sn, ALU.mult, par=True)
                    tt(x1, rt[0], rt[1], ALU.subtract)
                    t = tt(x2, rt[2], rt[3], ALU.add, par=True)
                    yield
                for i in range(5):
                    b = take()
                    for m in range(4):
                        tp = tr(b.ap[:, m * 128:(m + 1) * 128], QK[:, m, i * 128:(i + 1) * 128],
                                t, *(b.free if m == 0 else ()))
                    te = acp(QKT[:, i, :], b.ap[:, :], tp, par=True)
                    give(b, te)
                yield
                for j in range(2):
                    side(f"att{l}{j}", heads(j, tp, te))

            def heads(j, t_read, te):
                SC = ar(O_ATT + 1024 * j, 4, 256)
                rows = slice(64 * j, 64 * j + 64)
                mx, su, es = [sm[:, 480 + 8 * i + 4 * j:484 + 8 * i + 4 * j] for i in range(3)]
                sink = r1[:, R1["sink"] + 4 * j:R1["sink"] + 4 * j + 4]
                t_pv = None
                for m in range(4):
                    kw = 128 if m == 0 else 256
                    k0 = max(0, m - 1) * 128
                    am = AM[:, 256 - kw:256]
                    for g in range(2):
                        b = take()
                        for u in range(2):
                            tp = mm(b.ap[:, u * 256:u * 256 + kw],
                                    [(QKT[rows, 2 * g + u, m * 128:(m + 1) * 128], QKT[rows, 4, k0:k0 + kw])],
                                    te, *b.free)
                        tv = stt(SC[:, 2 * g:2 * g + 2, 0:kw],
                                 b.ap.rearrange("p (u k) -> p u k", u=2)[:, :, 0:kw], 0.125,
                                 bc(am, 1, 2), ALU.mult, ALU.add, tp, t_read, par=g > 0)
                        give(b, tv)
                    s = SC[:, :, 0:kw]
                    red(mx, s, ALU.max)
                    tt(mx, mx, sink, ALU.max)
                    tt(es, sink, mx, ALU.subtract)
                    tv = tt(s, s, bc(mx, 2, kw), ALU.subtract, par=True)
                    ta = act(es, es, ACT.Exp, tv, par=True)
                    ta = act(s, s, ACT.Exp, tv, par=True)
                    yield
                    red(su, s, ALU.add, ta, par=True)
                    tt(su, su, es, ALU.add)
                    rec(su, su)
                    tv = tt(s, s, bc(su, 2, kw), ALU.mult)
                    yield
                    nk = kw // 128
                    for kt in range(nk):
                        b = take()
                        for i in range(4):
                            tp = tr(b.ap[:, i * 128:(i + 1) * 128], SC[:, i, kt * 128:(kt + 1) * 128], tv, *b.free)
                        te2 = acp(PT[:, kt * 2 + j, :], b.ap[:, :], tp, t_pv, par=True)
                        give(b, te2)
                    t_read = tp
                    yield
                    b = take()
                    tp = mm(b.ap[rows, :], [(AV[:, k0 // 128 + kt, rows], PT[:, kt * 2 + j, :]) for kt in range(nk)],
                            te2, *b.free)
                    t_pv = tp
                    te2 = vcp(MIX[rows, 0:4, m * 128:(m + 1) * 128], b.ap[rows, :].rearrange("p (i q) -> p i q", i=4),
                              tp, par=True)
                    give(b, te2)
                    yield

            def finish(o, gate, tile0):
                sq = E_.rearrange("p (a b) -> p a b", a=4)
                ss = sm[:, 512:528]
                tt(sq, o, o, ALU.mult)
                red(ss, E_.rearrange("p (h d) -> p h d", d=64), ALU.add)
                rstd(ss, 16, 1.0 / 64, 1e-6)
                for m in range(4):
                    q = o[:, m, :].rearrange("p (h d) -> p h d", d=64)
                    tt(q, q, bc(ss[:, 4 * m:4 * m + 4], 2, 64), ALU.mult)
                t = act(sq, gate, ACT.Tanh, V.now(), scale=0.5)
                stt(sq, sq, 1.0, gate, ALU.add, ALU.mult, t)
                t = stt(o, sq, 0.5, o, ALU.mult, ALU.mult)
                yield
                for k in range(2):
                    b = take()
                    for m in range(4):
                        tp = tr(b.ap[:, m * 128:(m + 1) * 128], o[:, m, k * 128:(k + 1) * 128], t, *b.free)
                    g = C1["gain"] + tile0 - 4 + k
                    te = ts(MIX[:, tile0 + k, :], b.ap[:, :], c1[:, g:g + 1], None, ALU.mult, None, tp)
                    give(b, te)
                yield

            def hgrn():
                join(t_gt[0])
                U_, AZ, LU = E_, XL, ACC.rearrange("p a b -> p (a b)")[:, 0:1024]
                W_ = ACC.rearrange("p a b -> p (a b)")[:, 1024:2048]
                act(AZ, Zb, ACT.Abs, V.now())
                act(U_, AZ, ACT.Exp, scale=-1.0)
                t = act(LU, U_, ACT.Ln, bias=1.0)
                ts(W_, U_, 1.0, None, ALU.add, None, t)
                rec(W_, W_)
                stt(KT, Zb, 0.0, U_, ALU.is_lt, ALU.max)
                tt(KT, KT, W_, ALU.mult)
                if l == 0:
                    stt(Zb, Zb, 0.0, LU, ALU.min, ALU.subtract)
                else:
                    l0, l1 = c1[:, C1["lb0"]:C1["lb0"] + 2], c1[:, C1["lb1"]:C1["lb1"] + 2]
                    mx, e0, e1, sm2, lb, om = [sm[:, 530 + 2 * i:532 + 2 * i] for i in range(6)]
                    tt(mx, l0, l1, ALU.max)
                    tt(e0, l0, mx, ALU.subtract)
                    t = tt(e1, l1, mx, ALU.subtract)
                    act(e0, e0, ACT.Exp, t)
                    t = act(e1, e1, ACT.Exp)
                    tt(sm2, e0, e1, ALU.add, t)
                    rec(sm2, sm2)
                    tt(e0, e0, sm2, ALU.mult)
                    tt(e1, e1, sm2, ALU.mult)
                    tt(lb, e0, e1, ALU.add)
                    tt(lb, lb, e0, ALU.subtract)
                    ts(om, lb, -1.0, 1.0, ALU.mult, ALU.add)
                    ts(W_, U_, -1.0, 1.0, ALU.mult, ALU.add)
                    stt(W_, Zb, 0.0, W_, ALU.is_ge, ALU.mult)
                    for i in range(2):
                        h = slice(512 * i, 512 * i + 512)
                        ts(KT[:, h], KT[:, h], om[:, i:i + 1], None, ALU.mult)
                        t = stt(U_[:, h], W_[:, h], om[:, i:i + 1], U_[:, h], ALU.mult, ALU.add)
                        t = act(U_[:, h], U_[:, h], ACT.Ln, t, bias=lb[:, i:i + 1])
                        tt(Zb[:, h], U_[:, h], LU[:, h], ALU.subtract, t)
                yield
                for i in range(8):
                    s = slice(128 * i, 128 * i + 128)
                    V(lambda e, s=s: e.tensor_tensor_scan(XL[:, s], ones, Zb[:, s], 0.0, ALU.mult, ALU.add))
                vcp(Zb, XL)
                CUM = Zb
                yield
                tk = V.now()
                for c in range(4):
                    b = take()
                    for h in HO:
                        pr, ti = (h % 2) * 64, h // 2
                        tp = mm(b.ap[:, h * 128:(h + 1) * 128],
                                [(KT3[pr:pr + 64, ti, c * 128:(c + 1) * 128], BQ3[pr:pr + 64, ti, c * 128:(c + 1) * 128])],
                                tk, rowsw(h), *b.free)
                    te = tt(ACC[:, c, :].rearrange("p (h t) -> p h t", h=4),
                            b.ap.rearrange("p (h t) -> p h t", h=4), bc(ident, 1, 4), ALU.mult, tp)
                    give(b, te)
                yield
                for i in range(2):
                    side(f"levels{l}{i}", levels(i, V.now(), PE.now()))
                side(f"hgrn_b{l}", hgrn_b(), (f"levels{l}0", f"levels{l}1"))

            def levels(i, t0, tp):
                sl = slice(512 * i, 512 * i + 512)
                X3, A4 = XL[:, sl], ACC.rearrange("p c (i h t) -> p c i h t", i=2, h=2)[:, :, i]
                for lv in range(7):
                    hb = 1 << lv

                    def halves(z):
                        v = z[:, sl].rearrange("p (n u b) -> p n u b", u=2, b=hb)
                        return v[:, :, 0, :], v[:, :, 1, :]
                    cf, cs = halves(Zb)
                    ef, es = halves(E_)
                    xf, xs = halves(XL)
                    qf, qs = halves(BQ)
                    kf, ks = halves(KT)
                    ref = cf[:, :, hb - 1:hb].to_broadcast([128, 256 // hb, hb])
                    tt(es, cs, ref, ALU.subtract, t0)
                    t = tt(ef, ref, cf, ALU.subtract, par=True)
                    t = act(E_[:, sl], E_[:, sl], ACT.Exp, t, par=True)
                    yield
                    tt(xs, qs, es, ALU.mult, t, tp, par=True)
                    t0 = tx = tt(xf, kf, ef, ALU.mult, t, tp, par=True)
                    yield
                    mk = LV[lv].bitcast(I32).unsqueeze(1).unsqueeze(1).to_broadcast([128, 2, 2, 128])
                    for c in range(0, 4, 2):
                        b = take()
                        for h in range(2):
                            for u in range(2):
                                x = X3[64 * h:64 * h + 64, (c + u) * 128:(c + u + 1) * 128]
                                tp = mm(b.ap[:, (2 * u + h) * 128:(2 * u + h + 1) * 128], [(x, x)], tx,
                                        PE.now() if h and not u else None, *b.free)
                        te = V(lambda e, c=c, b=b, mk=mk: e.copy_predicated(
                            A4[:, c:c + 2], mk, b.ap.rearrange("p (c h t) -> p c h t", c=2, h=2)), tp, par=True)
                        give(b, te)
                    yield

            def hgrn_b():
                CUM = Zb
                tp = PE.now()
                last = CUM.rearrange("p (n t) -> p n t", t=128)[:, :, 127:128]
                C8 = CUM.rearrange("p (n t) -> p n t", t=128)
                EL = sm[:, 544:552]
                t = act(E_, CUM, ACT.Exp, V.now())
                tt(BQ, BQ, E_, ALU.mult, t, tp)
                t1 = act(EL, last.rearrange("p n o -> p (n o)"), ACT.Exp)
                t = tt(E_.rearrange("p (n t) -> p n t", t=128), last.to_broadcast([128, 8, 128]), C8, ALU.subtract, t1)
                t = act(E_, E_, ACT.Exp, t)
                t = tt(KT, KT, E_, ALU.mult, t)
                V(lambda e: e.memset(ST, 0.0))
                yield
                KD = E_.rearrange("p (a b) -> p a b", a=4)
                for m in range(0, 4, 2):
                    b = take()
                    for u in range(4):
                        tp = tr(b.ap[:, u * 128:(u + 1) * 128],
                                KT3[:, u % 2, (m + u // 2) * 128:(m + u // 2) * 128 + 128], t, *b.free)
                    te = vcp(KD[:, m:m + 2, :], b.ap.rearrange("p (a b) -> p a b", a=2), tp)
                    give(b, te)
                yield
                OB = XL.rearrange("p (a b) -> p a b", a=4)
                for c in range(4):
                    b, b2 = take(), take()
                    ts_ = V.now()
                    for h in range(4):
                        hs = slice(64 * h, 64 * h + 64)
                        tp = mm(b.ap[:, hs], [(ACC[:, c, h * 128:(h + 1) * 128], BV3[:, c, hs])], ts_, *b.free)
                    for h in HO:
                        pr, ti = (h % 2) * 64, h // 2
                        tp = mm(b.ap[:, 256 + 64 * h:320 + 64 * h],
                                [(BQ3[pr:pr + 64, ti, c * 128:(c + 1) * 128], ST[pr:pr + 64, ti, :])], rowsw(h))
                    for h in range(4):
                        pr, ti = (h % 2) * 64, h // 2
                        hs = slice(64 * h, 64 * h + 64)
                        tq = mm(b2.ap[pr:pr + 64, ti * 64:ti * 64 + 64], [(KD[:, c, hs], BV3[:, c, hs])], *b2.free)
                    vcp(OB[:, c, :], b.ap[:, 0:256], tp)
                    te = tt(OB[:, c, :], OB[:, c, :], b.ap[:, 256:512], ALU.add)
                    give(b, te)
                    for ti in range(2):
                        te = stt(ST[:, ti, :], ST[:, ti, :], EL[:, 4 * ti + c:4 * ti + c + 1],
                                 b2.ap[:, ti * 64:ti * 64 + 64], ALU.mult, ALU.add, tq)
                    give(b2, te)
                    yield
                yield from finish(OB, BG3, 4)

            def gdn():
                join()
                tc = V.now()
                TOK = ar(O_ATT, 4, 768)
                for i in range(6):
                    b = take()
                    for m in range(4):
                        tp = tr(b.ap[:, m * 128:(m + 1) * 128], CT[:, i, m * 128:(m + 1) * 128], tc, *b.free)
                    te = acp(TOK[:, :, i * 128:(i + 1) * 128], b.ap.rearrange("p (m c) -> p m c", m=4), tp, par=i > 0)
                    give(b, te)
                yield
                tct = tp
                be, g, gx, gu = [sm[:, 120 + 16 * i:136 + 16 * i] for i in range(4)]
                v3 = lambda z: z.rearrange("p (m h) -> p m h", m=4)
                t = act(v3(be), CBA[:, :, 0:4], ACT.Tanh, te, scale=0.5)
                ts(be, be, 1.0, 0.5, ALU.add, ALU.mult, t)
                t = tt(v3(g), CBA[:, :, 4:8], bc(r1[:, R1["dtb"]:R1["dtb"] + 4], 1, 4), ALU.add)
                act(gu, g, ACT.Abs, t)
                act(gu, gu, ACT.Exp, scale=-1.0)
                t = act(gx[:, 0:4], r1[:, R1["alog"]:R1["alog"] + 4], ACT.Exp)
                t = act(gu, gu, ACT.Ln, bias=1.0)
                stt(g, g, 0.0, gu, ALU.max, ALU.add, t)
                tg = stt(v3(g), v3(g), -1.0, bc(gx[:, 0:4], 1, 4), ALU.mult, ALU.mult)
                yield
                Gc, Gl, eG, eL, eD = [sm[:, 184 + 16 * i:200 + 16 * i] for i in range(5)]
                b = take()
                for m in range(4):
                    mm(b.ap[:, m * 4:m * 4 + 4], [(U, v3(g)[:, m, :])], tg, *b.free)
                    tp = mm(b.ap[:, 16 + m * 4:20 + m * 4], [(ones, v3(g)[:, m, :])])
                vcp(Gc, b.ap[:, 0:16], tp)
                te = vcp(Gl, b.ap[:, 16:32])
                give(b, te)
                t = tt(eD, Gl, Gc, ALU.subtract)
                act(eG, Gc, ACT.Exp, t)
                act(eL, Gl, ACT.Exp)
                tx = act(eD, eD, ACT.Exp)
                G5 = ar(O_ATT + 3072, 4, 512)
                yield
                for m in range(4):
                    b = take()
                    for h in range(4):
                        tp = mm(b.ap[:, h * 128:(h + 1) * 128], [(v3(g)[:, m, h:h + 1].to_broadcast([128, 128]), U)],
                                tg, *b.free)
                    for h in range(4):
                        te = ts(G5[:, m, h * 128:(h + 1) * 128], b.ap[:, h * 128:(h + 1) * 128],
                                Gc[:, 4 * m + h:4 * m + h + 1], 0.0, ALU.subtract, ALU.min, tp, par=True)
                    give(b, te)
                yield
                ta = act(G5, G5, ACT.Exp, te)
                for m in range(4):
                    u = G5[:, m, :].rearrange("p (h t) -> p h t", h=4)
                    tt(u, u, bc(U, 1, 4), ALU.mult, ta, par=m > 0)
                yield
                ss = sm[:, 264:296]
                sq = ar(O_ATT + 7168, 512)
                for m in range(4):
                    tt(sq, TOK[:, m, 0:512], TOK[:, m, 0:512], ALU.mult, tx, tp)
                    red(ss[:, 8 * m:8 * m + 8], sq.rearrange("p (h d) -> p h d", d=64), ALU.add)
                rstd(ss, 32, 1.0, 1e-6)
                s3 = ss.rearrange("p (m h) -> p m h", m=4)
                ts(s3[:, :, 0:4], s3[:, :, 0:4], 0.125, None, ALU.mult)
                KB, QD, KG = [ar(O_C + 516 + 1024 * i, 4, 256) for i in range(3)]
                for m in range(4):
                    qk = TOK[:, m, 0:512].rearrange("p (h d) -> p h d", d=64)
                    tt(qk, qk, bc(ss[:, 8 * m:8 * m + 8], 2, 64), ALU.mult, tct)
                    hd = lambda z: z.rearrange("p (h d) -> p h d", d=64)
                    q, k, v = [hd(TOK[:, m, 256 * i:256 * i + 256]) for i in range(3)]
                    sl = slice(4 * m, 4 * m + 4)
                    tt(hd(KB[:, m, :]), k, bc(be[:, sl], 2, 64), ALU.mult)
                    tt(hd(QD[:, m, :]), q, bc(eG[:, sl], 2, 64), ALU.mult, par=True)
                    tt(hd(KG[:, m, :]), hd(KB[:, m, :]), bc(eG[:, sl], 2, 64), ALU.mult)
                    tt(v, v, bc(be[:, sl], 2, 64), ALU.mult, par=True)
                t = V.now()
                yield
                TR = X.rearrange("p m (a b) -> p m a b", b=128)
                for m in range(4):
                    for half in range(2):
                        b = take()
                        for u in range(4 - 2 * half):
                            src = ((TOK[:, m, 0:256], TOK[:, m, 256:512]), (KB[:, m, :], QD[:, m, :]))[half][u // 2]
                            tp = tr(b.ap[:, u * 128:(u + 1) * 128], src[:, (u % 2) * 128:(u % 2) * 128 + 128], t, *b.free)
                        k = 4 - 2 * half
                        te = acp(TR[:, m, 4 * half:4 * half + k, :],
                                 b.ap[:, 0:128 * k].rearrange("p (a b) -> p a b", a=k), tp, t, t_xs, par=True)
                        give(b, te)
                yield
                for m in range(4):
                    k = TOK[:, m, 256:512].rearrange("p (h d) -> p h d", d=64)
                    tt(k, k, bc(eD[:, 4 * m:4 * m + 4], 2, 64), ALU.mult, tp, par=True)
                AT = ar(O_ATT + 5120, 4, 512)
                TT = X[:, :, 512:1024]
                TM = X[:, :, 0:512]
                XM = KB.rearrange("p a b -> p (a b)").rearrange("p (a b) -> p a b", a=2)
                for m in range(4):
                    for which in range(2):
                        b = take()
                        for h in HO:
                            pr, ti = (h % 2) * 64, h // 2
                            tp = mm(b.ap[:, h * 128:(h + 1) * 128],
                                    [(TR[pr:pr + 64, m, 2 + ti, :], TR[pr:pr + 64, m, (4 if which == 0 else 0) + ti, :])],
                                    te, rowsw(h), *b.free)
                        dst = AT if which == 0 else G5
                        te2 = tt(dst[:, m, :], b.ap[:, :], G5[:, m, :], ALU.mult, tp)
                        give(b, te2)
                    yield
                MA = [CIN[:, 0:512], ar(O_ATT + 7168, 512)]
                tb_ = []
                for m in range(4):
                    a4, t4 = [z[:, m, :].rearrange("p (h t) -> p h t", h=4) for z in (AT, TT)]
                    stt(t4, a4, -1.0, bc(LV[0], 1, 4), ALU.mult, ALU.mult)
                    t = tt(t4, t4, bc(ident, 1, 4), ALU.add)
                    b = take()
                    for h in range(4):
                        tp = tr(b.ap[:, h * 128:(h + 1) * 128], TT[:, m, h * 128:(h + 1) * 128], t, *b.free)
                    te = acp(TM[:, m, :], b.ap[:, :], tp)
                    give(b, te)
                yield
                for i in range(2):
                    side(f"inv{l}{i}", inverse(i, [A.now()] * 4, AT, TT, TM, XM, MA))
                side(f"gdn_b{l}", gdn_b(AT, TT, KB, QD, KG, G5, eL, TOK), (f"inv{l}0", f"inv{l}1"))

            def inverse(i, tT, AT, TT, TM, XM, MA):
                tma = tx2 = None
                for lv in range(1, 7):
                    for m in (i, i + 2):
                        a4 = AT[:, m, :].rearrange("p (h t) -> p h t", h=4)
                        ma = MA[i]
                        t = stt(ma.rearrange("p (h t) -> p h t", h=4), a4, -1.0, bc(LV[lv], 1, 4),
                                ALU.mult, ALU.mult, tma)
                        b = take()
                        for h in range(4):
                            hs = slice(h * 128, h * 128 + 128)
                            tp = mm(b.ap[:, hs], [(ma[:, hs], TM[:, m, hs])], t, tT[m], *b.free)
                        tma = tp
                        te = acp(XM[:, i, :], b.ap[:, :], tp, tx2, par=lv > 1)
                        give(b, te)
                        yield
                        b1, b2 = take(), take()
                        for h in range(4):
                            hs = slice(h * 128, h * 128 + 128)
                            tp = mm(b1.ap[:, hs], [(XM[:, i, hs], TT[:, m, hs])], te, *b1.free)
                            if lv < 6:
                                tp = mm(b2.ap[:, hs], [(TT[:, m, hs], XM[:, i, hs])], *b2.free)
                        if lv < 6:
                            te = tt(TM[:, m, :], TM[:, m, :], b2.ap[:, :], ALU.add, tp, par=lv > 1)
                            give(b2, te)
                        else:
                            give(b2, *b2.free)
                        te = tt(TT[:, m, :], TT[:, m, :], b1.ap[:, :], ALU.add, tp, par=lv > 1)
                        give(b1, te)
                        tx2 = tp
                        tT[m] = te
                        yield

            def gdn_b(AT, TT, KB, QD, KG, G5, eL, TOK):
                t_tt = V.now()
                NW = KB
                for m in range(4):
                    b = take()
                    for h in range(4):
                        pr, ti = (h % 2) * 64, h // 2
                        tp = mm(b.ap[pr:pr + 64, ti * 128:ti * 128 + 128],
                                [(KG[:, m, 64 * h:64 * h + 64], TT[:, m, h * 128:h * 128 + 128])], t_tt, *b.free)
                    te = ts(NW[:, m, :], b.ap[:, 0:256], -1.0, None, ALU.mult, None, tp)
                    give(b, te)
                yield
                SG = ar(O_C, 2, 64)
                VN = ar(O_C + 128, 256)
                QT_ = ar(O_ATT + 5120, 4, 2, 128)
                for half in range(2):
                    b = take()
                    for u in range(4):
                        m, ti = 2 * half + u // 2, u % 2
                        tp = tr(b.ap[:, u * 128:(u + 1) * 128], QD[:, m, ti * 128:(ti + 1) * 128], *b.free)
                    te = acp(QT_[:, 2 * half:2 * half + 2, :, :], b.ap.rearrange("p (m a b) -> p m a b", m=2, a=2), tp,
                             V.now())
                    give(b, te)
                t_qt = te
                V(lambda e: e.memset(SG, 0.0), PE.now())
                yield
                for m in range(4):
                    t = V.now()
                    b, b2, b3 = take(), take(), take()
                    for h in range(4):
                        mm(b.ap[:, 64 * h:64 * h + 64],
                           [(TT[:, m, h * 128:h * 128 + 128], TOK[:, m, 512 + 64 * h:576 + 64 * h])], t, *b.free)
                    for h in HO:
                        pr, ti = (h % 2) * 64, h // 2
                        mm(b.ap[:, 256 + 64 * h:320 + 64 * h],
                           [(NW[pr:pr + 64, m, ti * 128:ti * 128 + 128], SG[pr:pr + 64, ti, :])], rowsw(h))
                        tp = mm(b2.ap[:, 256 + 64 * h:320 + 64 * h],
                                [(QT_[pr:pr + 64, m, ti, :], SG[pr:pr + 64, ti, :])], t_qt, *b2.free)
                    vcp(VN, b.ap[:, 0:256], tp)
                    te = tt(VN, VN, b.ap[:, 256:512], ALU.add)
                    give(b, te)
                    yield
                    for h in range(4):
                        pr, ti = (h % 2) * 64, h // 2
                        hs = slice(64 * h, 64 * h + 64)
                        mm(b2.ap[:, hs], [(G5[:, m, h * 128:h * 128 + 128], VN[:, hs])], te)
                        tp = mm(b3.ap[pr:pr + 64, ti * 64:ti * 64 + 64], [(TOK[:, m, 256 + 64 * h:320 + 64 * h], VN[:, hs])],
                                *b3.free)
                    vcp(TOK[:, m, 0:256], b2.ap[:, 0:256], tp)
                    te = tt(TOK[:, m, 0:256], TOK[:, m, 0:256], b2.ap[:, 256:512], ALU.add)
                    give(b2, te)
                    for h in range(4):
                        pr, ti = (h % 2) * 64, h // 2
                        te = stt(SG[pr:pr + 64, ti, :], SG[pr:pr + 64, ti, :],
                                 eL[pr:pr + 64, 4 * m + h:4 * m + h + 1],
                                 b3.ap[pr:pr + 64, ti * 64:ti * 64 + 64], ALU.mult, ALU.add, par=h > 0)
                    give(b3, te)
                    yield
                OC = KG
                t = vcp(OC, TOK[:, :, 0:256])
                yield from finish_c(OC)

            def finish_c(o):
                sq, sqf = ar(O_C + 516 + 1024, 4, 256), ar(O_C + 516 + 1024, 16, 64)
                ss = sm[:, 300:316]
                tt(sq, o, o, ALU.mult)
                red(ss, sqf, ALU.add)
                rstd(ss, 16, 1.0 / 64, 1e-6)
                for m in range(4):
                    q = o[:, m, :].rearrange("p (h d) -> p h d", d=64)
                    tt(q, q, bc(ss[:, 4 * m:4 * m + 4], 2, 64), ALU.mult)
                t = act(sq, CG, ACT.Tanh, V.now(), scale=0.5)
                stt(sq, sq, 1.0, CG, ALU.add, ALU.mult, t)
                t = stt(o, sq, 0.5, o, ALU.mult, ALU.mult)
                yield
                for k in range(2):
                    b = take()
                    for m in range(4):
                        tp = tr(b.ap[:, m * 128:(m + 1) * 128], o[:, m, k * 128:(k + 1) * 128], t, *b.free)
                    g = C1["gain"] + 2 + k
                    te = ts(MIX[:, 6 + k, :], b.ap[:, :], c1[:, g:g + 1], None, ALU.mult, None, tp)
                    give(b, te)
                yield

            hw = sm[:, 560:584]
            ts(hw, c1[:, C1["conv"]:C1["conv"] + 24], 0.5, None, ALU.mult)
            V(lambda e: e.memset(CIN[:, 0:3], 0.0))
            gemm_t(W, 0, 512, 8, HT, need, ev0)
            gemm_t(W, 512, 256, 8, HT, need, ev1)
            then(lambda st: side(f"att{l}", attention()))
            gemm_c(W, 1792, 512, HT, 512, need, ev_c(0))
            gemm_c(W, 2304, 256, HT, 512, need, ev_c(4))
            gemm_t(W, 2560, 264, 8, HT, need, ev6)
            then(lambda st: side(f"gdn{l}", gdn(), (f"att{l}0", f"att{l}1")))
            gemm_c(W, 768, 512, HT, 512, need, ev2)
            gemm_t(W, 1280, 512, 8, HT, need, ev3)
            then(lambda st: side(f"hgrn{l}", hgrn()))
            jobs[:] = weave(jobs[:29], extra) + jobs[29:]
            memory(l)
            warm()
            norm_stats(X, 1e-6)
            xn = ar(0, 4, 1024)
            for m in range(4):
                scale_row(m)
            need.extend(to_ht(xn, mods[:, 8:16], mods[:, 0:8], ar(4096, 2, 512), V.now(), A.now()))
            join(t_xs)
            flush()
            drain()
            t_xr = s_misc[6].start(P, X[:, :, :], Xd, *fence())
            join(t_kv[l])

            def residual(g, scr, gt):
                tg = s_misc[8].start(P, gt, GTd[l, g * 1024:g * 1024 + 1024].partition_broadcast(128), V.now(), A.now(),
                                     PE.now(), t_gt[l])

                def mk(nb):
                    def ev(m, p, t):
                        tmp = scr[:, (m % 2), :]
                        t1 = tt(tmp, p, gt[:, nb * 512:(nb + 1) * 512], ALU.mult, t, tg)
                        xx = X[:, m, nb * 512:(nb + 1) * 512]
                        tt(xx, xx, tmp, ALU.add, t_xr)
                        return (t1,)
                    return ev
                return mk
            rs = residual(0, ar(0, 2, 512), ar(1024, 1024))
            for nb in range(2):
                gemm_t(T["w_out"][l], nb * 512, 512, 8, MIX, (), rs(nb))
            flush()
            join()
            need = []
            H2 = ar(0, 22, 512)
            t_gate, t_up = {}, {}

            def ev_gate(c0):
                def ev(c, p, t):
                    t_gate[c0 + c] = act(H2[:, c0 + c, :], p, ACT.Silu, t, par=True)
                    return (t_gate[c0 + c],)
                return ev

            def ev_up(c0):
                def ev(c, p, t):
                    h = H2[:, c0 + c, :]
                    t_up[c0 + c] = tt(h, h, p, ALU.mult, t, t_gate[c0 + c], par=True)
                    return (t_up[c0 + c],)
                return ev
            for nb in range(6):
                nw = min(512, FF - nb * 512)
                gemm_c(T["w_gate"][l], nb * 512, nw, HT, 512, need, ev_gate(4 * nb))
                gemm_c(T["w_up"][l], nb * 512, nw, HT, 512, need, ev_up(4 * nb))
            if l == 0:
                own, jobs[:] = list(jobs), []
                ada(1, range(12), [ar(14336 + 512 * i, 512) for i in range(4)])
                jobs[:] = weave(own, list(jobs))
            rs = residual(1, ar(11264, 2, 512), ar(12288, 1024))
            for nb in range(2):
                gemm_t(T["w_down"][l], nb * 512, 512, 22, H2, lambda k0: (t_up[k0 + 1],), rs(nb))
            warm()
            norm_stats(X, 1e-6)
            for m in range(4):
                scale_row(m)
            need.extend(to_ht(xn, mods[:, 32:40], mods[:, 24:32], ar(4096, 2, 512), V.now(), A.now()))
            join()
            flush()
            join()

        def second(l):
            lam_init = 0.8 - 0.6 * math.exp(-0.3 * l)
            t1 = s_misc[4].start(P, c2[:, :], T["c2"][l], V.now(), A.now())
            t2 = s_misc[5].start(P, r2[:, :], T["r2"][l].partition_broadcast(128), V.now(), A.now())
            join(t1, t2)
            need = []
            t_xs = s_misc[6].start(P, Xd, X[:, :, :], V.now(), A.now())
            W = T["w_in_2"][l]
            XS = ar(0, 4, 2048)
            Y = ar(8192, 4, 2048)
            BT = X[:, 0:2, :].rearrange("p a (b c) -> p (a b) c", c=512)
            CTt = X[:, 2:4, :].rearrange("p a (b c) -> p (a b) c", c=512)
            BTK = ar(16384, 4, 512)
            STt = ar(18432, 4, 512)
            R4 = 20480
            CV = [ar(R4 + 520 * i, 516) for i in range(2)]
            CO = [ar(R4 + 1040 + 512 * i, 512) for i in range(4)]
            hw = sm[:, 80:80 + 144]
            ts(hw, c2[:, 0:144], 0.5, None, ALU.mult)
            for i in range(2):
                V(lambda e, i=i: e.memset(CV[i][:, 0:2], 0.0))
                V(lambda e, i=i: e.memset(CV[i][:, 514:516], 0.0))
            st = dict(co=[None] * 4, cv=[V.now(), V.now()], n=0)

            def ev_x(c0):
                def ev(c, p, t):
                    i = c0 + c
                    cv, co = CV[i % 2], CO[i % 4]
                    while st["n"] < i - 1:
                        pump(True)
                    tf = acp(cv[:, 2:514], p, t, st["cv"][i % 2], par=True)

                    def conv():
                        ts(co, cv[:, 0:512], hw[:, 5 * i:5 * i + 1], hw[:, 120 + i:121 + i], ALU.mult, ALU.add, tf,
                           st["co"][i % 4])
                        for j in range(1, 5):
                            tv = stt(co, cv[:, j:j + 512], hw[:, 5 * i + j:5 * i + j + 1], co, ALU.mult, ALU.add)
                        yield
                        ta = act(cv[:, 2:514], co, ACT.Tanh, tv, par=True)
                        yield
                        dst = co if i < 16 else (BT if i < 20 else CTt)[:, i % 4, :]
                        tv = stt(dst, cv[:, 2:514], 1.0, co, ALU.add, ALU.mult, ta, par=True)
                        st["cv"][i % 2] = tv
                        st["co"][i % 4] = tv
                        st["n"] += 1
                        yield
                        if i < 20:
                            b = take()
                            for m in range(4):
                                tp = tr(b.ap[:, m * 128:(m + 1) * 128], dst[:, m * 128:(m + 1) * 128], tv, *b.free)
                            o = (XS[:, :, i * 128:(i + 1) * 128] if i < 16 else BTK[:, :, (i - 16) * 128:(i - 15) * 128])
                            te = acp(o, b.ap.rearrange("p (m c) -> p m c", m=4), tp, par=True)
                            give(b, te)
                            if i < 16:
                                st["co"][i % 4] = tp
                    side("conv", conv())
                    return (tf,)
                return ev

            for nb in range(6):
                gemm_c(W, 2048 + nb * 512, 512, HT, 512, need, ev_x(4 * nb))
            DT = sm[:, 224:480].rearrange("p (m h) -> p m h", m=4)

            def ev_dt(m, p, t):
                return (tt(DT[:, m, :], p, r2[:, R2["dtb"]:R2["dtb"] + 64], ALU.add, t),)
            gemm_t(W, 5120, 64, 8, HT, need, ev_dt)
            WDt = ar(R4 + 512, 4, 64)

            ES = [ar(R4 + 1024 * i, 2, 4, 128) for i in range(2)]
            TB = ar(R4 + 1536, 512)
            AA = ar(R4 + 2688, 4, 64)
            NC = ar(R4 + 2944, 4, 64)
            AL = ar(R4 + 2432, 4, 64)
            CB = ar(R4 + 2048, 128)
            BL = ar(R4 + 2176, 4, 64)

            def ssd():
                join()
                dt = sm[:, 224:480]
                u = AL.rearrange("p a b -> p (a b)")
                act(u, dt, ACT.Abs)
                act(u, u, ACT.Exp, scale=-1.0)
                act(NC[:, 0, :], r2[:, R2["alog"]:R2["alog"] + 64], ACT.Exp)
                t = act(u, u, ACT.Ln, bias=1.0)
                stt(dt, dt, 0.0, u, ALU.max, ALU.add, t)
                t_aa = t = stt(AA, DT, -1.0, bc(NC[:, 0, :], 1, 4), ALU.mult, ALU.mult)
                yield
                b = take()
                for m in range(4):
                    mm(b.ap[:, m * 64:m * 64 + 32], [(U, AA[:, m, 0:32])], t, *b.free)
                    mm(b.ap[:, m * 64 + 32:m * 64 + 64], [(Lr, AA[:, m, 32:64])])
                    tp = mm(b.ap[:, 256 + m * 64:256 + m * 64 + 64], [(ones, AA[:, m, :])])
                ts(NC, b.ap[:, 0:256].rearrange("p (a b) -> p a b", a=4), -1.0, None, ALU.mult, None, tp)
                te = vcp(AL, b.ap[:, 256:512].rearrange("p (a b) -> p a b", a=4))
                give(b, te)
                t = ts(BL, DT, 1e-38, None, ALU.max)
                t = act(BL, BL, ACT.Ln, t)
                t_bi = tt(BL, BL, NC, ALU.add, t)
                t_e = [None, None]
                r3 = lambda z: z.rearrange("p (h d) -> p h d", h=8)
                prev = None
                for n in range(33):
                    if n < 32:
                        m, g, q = n // 8, n // 2 % 4, n % 2
                        if q == 0:
                            b = take()
                            tc = mm(b.ap[:, 0:128], [(BT[:, g, m * 128:(m + 1) * 128],
                                                      CTt[:, g, m * 128:(m + 1) * 128])], *b.free)
                            bcb = b
                        E2 = ES[n % 2]
                        for d, tri in enumerate((U, Lr)):
                            h0 = 32 * d + 8 * g + 4 * q
                            b = take()
                            PE(lambda e, b=b, d=d: e.matmul(b.ap.rearrange("p (h t) -> p h t", h=4), NFr[0][:, :],
                                                            bc(NFr[1 + d][:, :], 1, 4), start=True, stop=False),
                               t_aa, *b.free, inc=False, us=0.21)
                            for h in range(4):
                                tp = PE(lambda e, b=b, h=h, h0=h0, m=m, tri=tri: e.matmul(
                                    b.ap[:, h * 128:(h + 1) * 128], AA[:, m, h0 + h:h0 + h + 1].to_broadcast([128, 128]),
                                    tri, start=False, stop=h == 3), inc=h == 3, us=0.21)
                            for h in range(4):
                                te = act(E2[:, d, h, :], b.ap[:, h * 128:(h + 1) * 128], ACT.Exp, tp, t_bi, t_e[n % 2],
                                         bias=BL[:, m, h0 + h:h0 + h + 1], par=True)
                            give(b, te)
                            if d == 0:
                                yield
                        ta = te
                    if prev is not None:
                        pn, pm, pg, pq, pE, pta = prev
                        if pq == 0:
                            tcb = vcp(CB, pcb.ap[:, 0:128], ptc)
                            give(pcb, tcb)
                        tt(pE[:, 0], pE[:, 0], pE[:, 1], ALU.add, pta)
                        tv = tt(pE[:, 0, :, :], pE[:, 0, :, :], bc(CB, 1, 4), ALU.mult)
                        yield
                        if pq == 0:
                            by = take()
                        for h in range(4):
                            hs = slice(256 * pq + 64 * h, 256 * pq + 64 * h + 64)
                            xs_ = XS[:, pm, 512 * pg + 256 * pq + 64 * h:512 * pg + 256 * pq + 64 * h + 64]
                            tp = mm(by.ap[:, hs], [(pE[:, 0, h, :], xs_)], tv, *by.free)
                        t_e[pn % 2] = tp
                        if pq == 1:
                            xg = XS[:, pm, 512 * pg:512 * pg + 512]
                            yg = Y[:, pm, 512 * pg:512 * pg + 512]
                            tt(r3(yg), r3(xg), bc(r2[:, R2["skip"] + 8 * pg:R2["skip"] + 8 * pg + 8], 2, 64), ALU.mult)
                            te = tt(yg, yg, by.ap[:, :], ALU.add, tp)
                            give(by, te)
                    if n < 32:
                        prev = (n, m, g, q, E2, ta)
                        if q == 0:
                            pcb, ptc = bcb, tc
                    yield
                join()
                WD = WDt
                t = tt(WD, AL, NC, ALU.add)
                t = act(WD, WD, ACT.Exp, t)
                tt(WD, WD, DT, ALU.mult, t)
                AC = NC
                t = act(AC, AC, ACT.Exp, scale=-1.0)
                t = act(AL, AL, ACT.Exp)
                XW = [ar(R4 + 1024 * i, 512) for i in range(2)]
                t_w = [None, None]
                n = 0
                for d in range(2):
                    order = range(4) if d == 0 else range(3, -1, -1)
                    for ci, m in enumerate(order):
                        for g in range(4):
                            hh = slice(32 * d + 8 * g, 32 * d + 8 * g + 8)
                            xw = XW[n % 2]
                            tv = tt(r3(xw), r3(XS[:, m, 512 * g:512 * g + 512]), bc(WD[:, m, hh], 2, 64), ALU.mult,
                                    t, t_w[n % 2])
                            if ci:
                                b = take()
                                tp = mm(b.ap[:, :], [(CTt[:, g, m * 128:(m + 1) * 128], STt[:, g, :])], t_st[g], *b.free)
                                yg = Y[:, m, 512 * g:512 * g + 512]
                                te = tt(r3(TB), r3(b.ap), bc(AC[:, m, hh], 2, 64), ALU.mult, tp)
                                give(b, te)
                                tt(yg, yg, TB, ALU.add)
                            if ci < 3:
                                b = take()
                                tq = mm(b.ap[:, :], [(BTK[:, m, g * 128:(g + 1) * 128], xw)], tv, *b.free)
                                t_w[n % 2] = tq
                                sg = STt[:, g, :]
                                if ci == 0:
                                    te = vcp(sg, b.ap[:, :], tq)
                                else:
                                    tt(r3(sg), r3(sg), bc(AL[:, m, hh], 2, 64), ALU.mult)
                                    te = tt(sg, sg, b.ap[:, :], ALU.add, tq)
                                give(b, te)
                                if ci == 0 and g == 0:
                                    t_st = [None] * 4
                                t_st[g] = te
                            n += 1
                            yield

            def start_ssd(st_):
                while st["n"] < 24 or any(x[0] == "conv" for x in sides):
                    pump(True)
                side(f"ssd{l}", ssd())
            then(start_ssd)
            STG = ar(23680, 3, 512)
            n_stg = [0]

            def ev_store(dst, n0, kind):
                def ev(m, p, t):
                    i = n_stg[0] % 3
                    n_stg[0] += 1
                    g = STG[:, i, :]
                    free = (s_st[i].sem, s_st[i].n) if s_st[i].n else None
                    if kind == "silu":
                        t = act(g, p, ACT.Tanh, t, free, scale=0.5)
                        t = stt(g, g, 1.0, p, ALU.add, ALU.mult, t)
                        rel = t
                        t = ts(g, g, 0.5, None, ALU.mult)
                    else:
                        rel = t = tt(g, p, GBL, ALU.add, t, free, t_gb[0])
                        t = act(g, g, ACT.Tanh, t, scale=0.5)
                        t = ts(g, g, 1.0, 0.5, ALU.add, ALU.mult, t)
                    s_st[i].start(P, dst[m, :, n0:n0 + 512], g, t)
                    return (rel,)
                return ev
            GBL = ar(25216, 512)
            GB_ = ar(24704, 2, 512)
            n_gb, t_gb = [0], [None]
            for nb in range(4):
                gemm_t(W, nb * 512, 512, 8, HT, need, ev_store(Zd, nb * 512, "silu"))
            for nb in range(6):
                def gbl(st, nb=nb):
                    n_gb[0] = nb
                    t_gb[0] = s_misc[8].start(
                        P, GBL, T["gateb"][l][nb * 512:(nb + 1) * 512].partition_broadcast(128), V.now())
                then(gbl)
                gemm_t(W, 11328 + nb * 512, 512, 8, HT, need, ev_store(Gd, nb * 512, "sig"))
            for nb in range(2):
                gemm_t(W, 8256 + nb * 512, 512, 8, HT, need, ev_store(Dg, nb * 512, "silu"))
            for nb in range(2):
                gemm_t(W, 10304 + nb * 512, 512, 8, HT, need, ev_store(Cg, nb * 512, "silu"))
            warm()
            need.extend(to_ht(X, None, None, ar(0, 2, 512)))
            join(t_xs)
            flush()
            drain()
            join()
            stored = [(s.sem, s.n) for s in s_st[0:3] if s.n]
            ZT = ar(18432, 2, 2048)
            YT = ar(0, 16, 512)
            SSY = sm[:, 604:608]
            start = fence()

            def gated():
                tq = [None, None]
                for m in range(4):
                    zt = ZT[:, m % 2, :]
                    tz = s_misc[8 + m % 2].start(P, zt, Zd[m], *stored, tq[m % 2], *(start if m < 2 else ()))
                    tv = tt(Y[:, m, :], Y[:, m, :], zt, ALU.mult, tz)
                    tq[m % 2] = act(zt, Y[:, m, :], ACT.Square, tv, acc=SSY[:, m:m + 1])
                    yield
                t = ts(SSY, SSY, 1.0 / 2048, 1e-5, ALU.mult, ALU.add, A.now())
                t = act(SSY, SSY, ACT.Sqrt, t)
                rec(SSY, SSY, t)
                yield
                w = c2[:, C2["ssd"]:C2["ssd"] + 16]
                for k in range(0, 16, 2):
                    turn(Y, YT, (k, k + 1), w, tv)
                    yield
                join()
            side(f"gated{l}", gated())

            MG = HF[:, 1, :].rearrange("p (m a) -> p m a", m=4)

            def branch(w, kt, lhs, which, bufs, scale=None):
                tiles = [(nb, m) for nb in range(2) for m in range(4)]
                nbuf = len(bufs)
                tg = {}

                def load(j, *w_):
                    if j < 8:
                        nb, m = tiles[j]
                        tg[j] = s_g[j % nbuf].start(P, bufs[j % nbuf], Gd[
                            m, :, which * 1024 + nb * 512:which * 1024 + nb * 512 + 512], *stored, *w_)
                for j in range(nbuf):
                    load(j, V.now(), PE.now(), A.now())
                for nb in range(2):
                    def ev(m, p, t, nb=nb):
                        j = 4 * nb + m
                        g = bufs[j % nbuf]
                        mg = MG[:, m, nb * 512:(nb + 1) * 512]
                        if scale is not None:
                            r = last = stt(mg, p, scale[:, m:m + 1], g, ALU.mult, ALU.mult, t, tg[j], par=True)
                        else:
                            r = tt(g, p, g, ALU.mult, t, tg[j], par=True)
                            last = tt(mg, mg, g, ALU.add)
                        load(j + nbuf, last)
                        return (r,)
                    gemm_t(w, nb * 512, 512, kt, lhs, (), ev)

            QT = ar(8192, 8, 512)
            KT = ar(12288, 8, 512)
            DV = ar(16384, 4, 1024)
            OD = HF[:, 0, :].rearrange("p (m a) -> p m a", m=4)
            CQ = X.rearrange("p a (b c) -> p (a b) c", c=512)
            RT = ar(R4, 2, 512)
            RM = ar(R4 + 1024, 4, 256)
            n_rt, n_turned = [0], [0]
            t_rt = [None, None]

            def ev_rope(dst, t0):
                def ev(m, p, t):
                    i = n_rt[0] % 2
                    while n_turned[0] < n_rt[0] - 1:
                        pump(True)
                    n_rt[0] += 1
                    q = p.rearrange("p (h u d) -> p h u d", u=2, d=32)
                    o = RT[:, i, :].rearrange("p (h u d) -> p h u d", u=2, d=32)
                    a, b_ = [RM[:, j, :].rearrange("p (h d) -> p h d", d=32) for j in range(2)]
                    cs, sn = bc(tabs[:, m, 16:48], 1, 8), bc(tabs[:, m, 48:80], 1, 8)
                    tt(a, q[:, :, 0, :], cs, ALU.mult, t)
                    tt(b_, q[:, :, 1, :], sn, ALU.mult, par=True)
                    a2, b2 = [RM[:, 2 + j, :].rearrange("p (h d) -> p h d", d=32) for j in range(2)]
                    tt(a2, q[:, :, 0, :], sn, ALU.mult, par=True)
                    tr_ = tt(b2, q[:, :, 1, :], cs, ALU.mult, par=True)
                    tt(o[:, :, 0, :], a, b_, ALU.subtract, t_rt[i])
                    tv = tt(o[:, :, 1, :], a2, b2, ALU.add, par=True)

                    def later():
                        b = take()
                        for k in range(4):
                            tp = tr(b.ap[:, k * 128:(k + 1) * 128], RT[:, i, k * 128:(k + 1) * 128], tv, *b.free)
                        te = acp(dst[:, t0:t0 + 4, m * 128:(m + 1) * 128], b.ap.rearrange("p (k c) -> p k c", k=4), tp)
                        give(b, te)
                        t_rt[i] = tp
                        n_turned[0] += 1
                        return
                        yield
                    side("later", later())
                    return (tr_,)
                return ev
            for nb in range(2):
                gemm_c(W, 9280 + nb * 512, 512, HT, 512, need,
                       lambda c, p, t, nb=nb: (acp(CQ[:, 4 * nb + c, :], p, t, par=True),))

            def wait_gated(st_):
                while f"gated{l}" not in done:
                    pump(True)
            then(wait_gated)
            for nb in range(2):
                gemm_t(W, 5184 + nb * 512, 512, 8, HT, need, ev_rope(QT, 4 * nb))
            for nb in range(2):
                gemm_t(W, 6208 + nb * 512, 512, 8, HT, need, ev_rope(KT, 4 * nb))

            def ev_dv(n0):
                return lambda m, p, t: (acp(DV[:, m, n0:n0 + 512], p, t, par=True),)
            for nb in range(2):
                gemm_t(W, 7232 + nb * 512, 512, 8, HT, need, ev_dv(nb * 512))

            def diff():
                join()
                PB = ar(R4, 3, 1024)
                WT = ar(R4 + 3072, 2, 512)
                lm = sm[:, 80:340]
                la = r2[:, R2["lam"]:R2["lam"] + 256]
                tt(lm[:, 0:64], la[:, 0:64], la[:, 64:128], ALU.mult)
                red(lm[:, 256:257], lm[:, 0:64], ALU.add)
                tt(lm[:, 0:64], la[:, 128:192], la[:, 192:256], ALU.mult)
                t = red(lm[:, 257:258], lm[:, 0:64], ALU.add)
                t = act(lm[:, 256:258], lm[:, 256:258], ACT.Exp, t)
                lam = lm[:, 258:259]
                tt(lam, lm[:, 256:257], lm[:, 257:258], ALU.subtract, t)
                ts(lam, lam, lam_init, None, ALU.add)
                mx = sm[:, 344:352].rearrange("p (a b) -> p a b", a=4)
                su = sm[:, 352:360].rearrange("p (a b) -> p a b", a=4)
                st_ = {}
                units = [(h, m) for h in range(8) for m in range(4)]
                t_w = [None] * 3
                t_pt = [None, None]

                def front(n):
                    h, m = units[n]
                    i = n % 3
                    bs = [take(), take()]
                    mn = mx[:, n % 4, :]
                    for c in range(2):
                        tp = mm(bs[c].ap[:, :], [(QT[64 * c:64 * c + 64, h, m * 128:(m + 1) * 128],
                                                  KT[64 * c:64 * c + 64, h, :])], *bs[c].free)
                        red(mn[:, c:c + 1], bs[c].ap[:, :], ALU.max, tp, par=c > 0)
                    tv = ts(mn, mn, -0.125, None, ALU.mult)
                    for c in range(2):
                        ta = act(PB[:, i, c * 512:c * 512 + 512], bs[c].ap[:, :], ACT.Exp, tv, t_w[i], scale=0.125,
                                 bias=mn[:, c:c + 1], acc=su[:, n % 4, c:c + 1], par=True)
                        give(bs[c], ta)
                    s = su[:, n % 4, :]
                    rec(s, s, ta)
                    tt(s[:, 1:2], s[:, 1:2], lam, ALU.mult)
                    ts(PB[:, i, 512:1024], PB[:, i, 512:1024], s[:, 1:2], None, ALU.mult)
                    st_[n] = stt(PB[:, i, 0:512], PB[:, i, 0:512], s[:, 0:1], PB[:, i, 512:1024], ALU.mult, ALU.subtract)

                def mid(n):
                    i, j = n % 3, n % 2
                    b = take()
                    for k in range(4):
                        tp = tr(b.ap[:, k * 128:(k + 1) * 128], PB[:, i, k * 128:(k + 1) * 128], st_[n], *b.free)
                    t_w[i] = tp
                    te = acp(WT[:, j, :], b.ap[:, :], tp, t_pt[j], par=True)
                    give(b, te)
                    st_[n] = te

                def back(n):
                    h, m = units[n]
                    i = n % 2
                    b = take()
                    tp = mm(b.ap[:, 0:128], [(WT[:, i, k * 128:(k + 1) * 128], DV[:, k, h * 128:(h + 1) * 128])
                                             for k in range(4)], st_[n], *b.free)
                    t_pt[i] = tp
                    te = vcp(OD[:, m, h * 128:(h + 1) * 128], b.ap[:, 0:128], tp, par=True)
                    give(b, te)
                DGb = ar(12288, 4, 1024)
                for n in range(len(units) + 3):
                    if n == len(units):
                        tdg = s_misc[10].start(P, DGb, Dg.rearrange("m p n -> p m n"), PE.now(), *stored)
                    if n >= 3:
                        back(n - 3)
                    if 2 <= n < len(units) + 2:
                        mid(n - 2)
                    if n < len(units):
                        front(n)
                    yield
                so = sm[:, 80:112]
                sq = ar(8192, 4, 1024)
                t = V.now()
                for m in range(4):
                    ta = act(sq[:, m, :], OD[:, m, :], ACT.Square, t, PE.now(), par=True)
                    red(so[:, 8 * m:8 * m + 8], sq[:, m, :].rearrange("p (h d) -> p h d", h=8), ALU.add, ta, par=True)
                rstd(so, 32, 1.0 / 128, 1e-5)
                ts(so, so, 1.0 - lam_init, None, ALU.mult)
                yield
                while not br_done:
                    yield
                ld.append(s_misc[6].start(P, ar(16384, 4096), KVd[l], PE.now(), t_kv[l]))
                ld.append(s_misc[9].start(P, ar(0, 4, 1024), Cg.rearrange("m p n -> p m n"), PE.now(), *stored))
                o3 = OD.rearrange("p m (h d) -> p m h d", h=8)
                for m in range(4):
                    tt(o3[:, m], o3[:, m], bc(so[:, 8 * m:8 * m + 8], 2, 128), ALU.mult, par=m > 0)
                for m in range(4):
                    tt(OD[:, m, :], OD[:, m, :], DGb[:, m, :], ALU.mult, tdg, par=m > 0)
                yield
                YD = ar(8192, 8, 512)
                gain = c2[:, C2["diff"]:C2["diff"] + 1]
                t = V.now()
                for k in range(8):
                    b = take()
                    for m in range(4):
                        tp = tr(b.ap[:, m * 128:(m + 1) * 128], OD[:, m, k * 128:(k + 1) * 128], t, *b.free)
                    te = act(YD[:, k, :], b.ap[:, :], ACT.Copy, tp, scale=gain)
                    give(b, te)
                    if k % 2:
                        yield

            def start_diff(st_):
                while any(x[0] == "later" for x in sides):
                    pump(True)
                side(f"diff{l}", diff())
            then(start_diff)
            br_done, ld = [], []
            branch(T["w_br_ssd_2"][l], 16, YT, 0, [GB_[:, i, :] for i in range(2)], SSY)
            then(lambda st: br_done.append(1))
            flush()
            drain()
            join()

            OC = ar(0, 4, 1024)
            tkv, tcg = ld

            def cross(i):
                MK = ar(16384, 8, 256)
                MV = ar(18432, 2, 1024)
                PX = ar(20480 + 1024 * i, 4, 256)
                PXT = ar(22528 + 1024 * i, 2, 512)
                mx, su = sm[:, 80 + 8 * i:84 + 8 * i], sm[:, 84 + 8 * i:88 + 8 * i]
                tp = tpv = None
                for m in (i, i + 2):
                    for g in range(2):
                        b = take()
                        for u in range(2):
                            h = 2 * g + u
                            tq = mm(b.ap[:, u * 256:(u + 1) * 256],
                                    [(CQ[:, 2 * h + k, m * 128:(m + 1) * 128], MK[:, 2 * h + k, :]) for k in range(2)],
                                    tkv, *b.free)
                        v = b.ap.rearrange("p (u k) -> p u k", u=2)
                        red(mx[:, 2 * g:2 * g + 2], v, ALU.max, tq, par=g > 0)
                        tv = tt(PX[:, 2 * g:2 * g + 2, :], v, bc(mx[:, 2 * g:2 * g + 2], 2, 256), ALU.subtract, tp)
                        give(b, tv)
                    ta = act(PX, PX, ACT.Exp, tv, scale=1.0 / 16, par=True)
                    yield
                    red(su, PX, ALU.add, ta, par=True)
                    ts_ = rec(su, su)
                    for kt in range(2):
                        b = take()
                        for h in range(4):
                            tp = tr(b.ap[:, h * 128:(h + 1) * 128], PX[:, h, kt * 128:(kt + 1) * 128], ta, *b.free)
                        te = acp(PXT[:, kt, :], b.ap[:, :], tp, tpv, par=True)
                        give(b, te)
                    yield
                    for g in range(2):
                        b = take()
                        for u in range(2):
                            h = 2 * g + u
                            tpv = mm(b.ap[:, u * 256:(u + 1) * 256],
                                     [(PXT[:, kt, h * 128:(h + 1) * 128], MV[:, kt, h * 256:(h + 1) * 256])
                                      for kt in range(2)], te, *b.free)
                        for u in range(2):
                            h = 2 * g + u
                            oc = OC[:, m, h * 256:(h + 1) * 256]
                            te2 = stt(oc, b.ap[:, u * 256:(u + 1) * 256], su[:, h:h + 1], oc, ALU.mult, ALU.mult,
                                      tpv, tcg, ts_, par=True)
                        give(b, te2)
                    yield

            def cross_t():
                YC = ar(4096, 8, 512)
                t = V.now()
                for k in range(8):
                    b = take()
                    for m in range(4):
                        tp = tr(b.ap[:, m * 128:(m + 1) * 128], OC[:, m, k * 128:(k + 1) * 128], t, *b.free)
                    te = acp(YC[:, k, :], b.ap[:, :], tp)
                    give(b, te)
                    if k % 2:
                        yield
            for i in range(2):
                side(f"cross{l}{i}", cross(i))
            side(f"cross_t{l}", cross_t(), (f"cross{l}0", f"cross{l}1"))
            GBs = [ar(12288 + 512 * i, 512) for i in range(6)]
            branch(T["w_br_diff_2"][l], 8, ar(8192, 8, 512), 1, GBs)
            flush()
            drain()
            join()
            branch(T["w_br_cross_2"][l], 8, ar(4096, 8, 512), 2, GBs)
            flush()
            join()
            MGT = ar(12288, 8, 512)
            turn(MG, MGT, range(8))
            join()
            t_xr = s_misc[6].start(P, X[:, :, :], Xd, PE.now(), V.now(), A.now())
            LNG = ar(16384, 1024)
            LNB = ar(17408, 1024)
            t1 = s_misc[4].start(P, LNG, T["lng"][l].partition_broadcast(128), V.now(), A.now(), PE.now())
            t2 = s_misc[5].start(P, LNB, T["lnb"][l].partition_broadcast(128), V.now(), A.now(), PE.now())
            BS = sm[:, 80:128].rearrange("p (m u s) -> p m u s", m=4, u=2)
            MVr = sm[:, 128:136].rearrange("p (m s) -> p m s", m=4)

            def ev_o(nb):
                def ev(m, p, t):
                    xx = X[:, m, nb * 512:(nb + 1) * 512]
                    r = stt(xx, xx, ALPHA, p, ALU.mult, ALU.add, t, t_xr)
                    V(lambda e: e.bn_stats(BS[:, m, nb, :], xx))
                    return (r,)
                return ev
            for nb in range(2):
                gemm_t(T["w_out_2"][l], nb * 512, 512, 8, MGT, (), ev_o(nb))
            flush()
            for m in range(4):
                V(lambda e, m=m: e.bn_aggr(MVr[:, m, :], BS[:, m, :, :]))
            ts(MVr[:, :, 1], MVr[:, :, 1], 1e-5, None, ALU.add)
            t = act(MVr[:, :, 1], MVr[:, :, 1], ACT.Sqrt, V.now())
            rec(MVr[:, :, 1], MVr[:, :, 1], t)
            for m in range(4):
                ts(X[:, m, :], X[:, m, :], MVr[:, m, 0:1], MVr[:, m, 1:2], ALU.subtract, ALU.mult)
                tt(X[:, m, :], X[:, m, :], LNG, ALU.mult, t1)
                tt(X[:, m, :], X[:, m, :], LNB, ALU.add, t2)
            join()

        PARTS(first, second)
        t = s_misc[7].start(SP, out.rearrange("o (m p) d -> p (o m) d", p=128), X[:, :, :], V.now())
        SP.ops.append(([t] + [(s.sem, s.n) for s in s_st if s.n], None, None, 0))

        block = ctx.enter_context(nc.Block())

        @block.sync
        def _(e):
            SP.emit(e)

        @block.tensor
        def _(e):
            PE.emit(e)

        @block.vector
        def _(e):
            V.emit(e)

        @block.scalar
        def _(e):
            A.emit(e)

        @block.gpsimd
        def _(e):
            P.emit(e)


def PARTS(first, second):
    for l in range(2):
        first(l)
    for l in range(2):
        second(l)


def constants():
    import numpy as np
    r = np.arange(128)
    s, t = r[:, None], r[None, :]
    k = np.zeros((128, NK), np.float32)
    k[:, K_ID:K_ID + 128] = np.eye(128)
    k[:, K_U:K_U + 128] = s <= t
    k[:, K_L:K_L + 128] = s >= t
    k[:, K_NF:K_NF + 128] = np.where(s <= t, 0.0, -1e30)
    k[:, K_NB:K_NB + 128] = np.where(s >= t, 0.0, -1e30)
    k[:, K_ONE:K_ONE + 128] = 1.0
    k[:, K_AM:K_AM + 128] = np.where(t > s, 0.0, -1e30)
    for i in range(7):
        b = 1 << i
        k[:, K_LV + 128 * i:K_LV + 128 * i + 128] = (t // b == s // b + 1) & (t // (2 * b) == s // (2 * b))
    k[:, K_F8:K_F8 + 8] = 500000.0 ** (-np.arange(8, dtype=np.float64) * 2.0 / 16)
    k[:, K_F32:K_F32 + 32] = 10000.0 ** (-np.arange(0, 64, 2, dtype=np.float64) / 64)
    return k


def layout(i):
    import numpy as np
    cols = lambda v: np.ascontiguousarray(np.asarray(v).reshape(-1, 128).T)
    a = {k: np.asarray(v) for k, v in i.items()}
    o = {"cst": constants(), "x": a["x"], "c": cols(a["c"]),
         "pos": np.concatenate([cols(a["positions"]), cols(a["positions_2"])], 1)}
    c1, r1, c2, r2, gtb = [], [], [], [], []
    for l in range(2):
        conv = a["gdn_conv_w"][l].reshape(4, 6, 128).transpose(2, 1, 0).reshape(128, 24)
        hg, gd = a["hgrn_out_norm"][l], a["gdn_out_norm"][l]
        gain = np.stack([np.tile(hg, 2)] * 2 + [np.tile(gd, 2)] * 2, 1)
        c1.append(np.concatenate([cols(a["norm_mix"][l]), cols(a["norm_ffn"][l]), cols(a["ada_b"][l]),
                                  cols(a["hgrn_lb_logits"][0]), cols(a["hgrn_lb_logits"][1]), conv, gain], 1))
        r1.append(np.concatenate([a["attn_q_norm"][l], a["attn_k_norm"][l], a["attn_sinks"][l],
                                  a["gdn_a_log"][l], a["gdn_dt_bias"][l]]))
        cv2 = a["conv_w_2"][l].reshape(5, 24, 128).transpose(2, 1, 0).reshape(128, 120)
        c2.append(np.concatenate([cv2, cols(a["conv_b_2"][l]), cols(a["ssd_norm_w_2"][l]),
                                  cols(a["diff_norm_w_2"][l])], 1))
        r2.append(np.concatenate([a["dt_bias_2"][l].ravel(), a["a_log_2"][l].ravel(), a["d_skip_2"][l],
                                  a["diff_lam_2"][l].ravel()]))
        gtb.append(np.concatenate([a["ada_b"][l][2048:3072], a["ada_b"][l][5120:6144]]))
    o.update(c1=np.stack(c1), r1=np.stack(r1), c2=np.stack(c2), r2=np.stack(r2), gtb=np.stack(gtb))
    for n in ("ada_w", "w_in", "w_gate", "w_up", "w_down", "w_in_2", "w_br_ssd_2", "w_br_diff_2", "w_br_cross_2",
              "w_out_2"):
        o[n] = a[n]
    o["w_mem"] = a["w_mem_kv_2"]
    wo = a["w_out"]
    top = wo[:, 0:512].reshape(2, 2, 4, 64, 1024).transpose(0, 2, 1, 3, 4).reshape(2, 512, 1024)
    o["w_out"] = np.concatenate([top, wo[:, 512:]], 1)
    o["memT"] = np.ascontiguousarray(a["mem_2"][0].T.reshape(8, 128, 256).transpose(1, 0, 2))
    o["gateb"] = a["gate_b_2"].reshape(2, 3072)
    o["lng"], o["lnb"] = a["ln_g_2"], a["ln_b_2"]
    return o


def kernel(**inputs):
    import numpy as np
    import concourse.bacc as bacc
    from concourse.bass_utils import run_bass_kernel_spmd as run

    nc = bacc.Bacc("TRN2", target_bir_lowering=False, num_devices=1)
    arrays, T = {}, {}
    for name, v in layout(inputs).items():
        v = np.ascontiguousarray(v)
        arrays["in_" + name] = v
        T[name] = nc.dram_tensor("in_" + name, v.shape, mybir.dt.from_np(v.dtype), kind="ExternalInput").ap()
    out = nc.dram_tensor("out_0", (1, S, D), F32, kind="ExternalOutput").ap()
    program(nc, T, out)
    r = run(nc, [arrays], core_ids=[0])
    return r.results[0]["out_0"]
```
